# Optimizing a Trainium2 kernel written in Bass

```python
import math
import jax
import jax.numpy as jnp
from jax import lax
import numpy as np

D_MODEL = 2048
BATCH = 1
SEQ = 256
DEPTH = 2

N_META = 16
CHUNK = 64
Q_BLOCK = 128
NORM_EPS = 1e-6

A_HEADS = 8
A_HEAD_DIM = 128
A_Q_RANK = 512
A_KV_RANK = 256
IDX_HEADS = 16
IDX_DIM = 64
TOPK_MAX = 256
TOPK_FRAC = 4

B_HEADS = 8
B_HEAD_DIM = 128
CONV_K = 4

C_HEADS = 8
C_QK_DIM = 256
C_V_DIM = 512
ROT_BASE = 10000.0

D_FF = -(-8 * D_MODEL // (3 * 256)) * 256

A_WIDTH = A_HEADS * A_HEAD_DIM
B_WIDTH = B_HEADS * B_HEAD_DIM
HY_IN_SIZES = (A_Q_RANK, A_KV_RANK, IDX_DIM, IDX_HEADS, 3 * B_WIDTH, B_WIDTH, B_HEADS, B_HEADS)
HY_IN_COLS = sum(HY_IN_SIZES)
C_QK_WIDTH = C_HEADS * C_QK_DIM
C_V_WIDTH = C_HEADS * C_V_DIM
RET_IN_SIZES = (C_QK_WIDTH, C_QK_WIDTH, C_V_WIDTH, C_V_WIDTH)
RET_IN_COLS = sum(RET_IN_SIZES)
N_EVEN = (DEPTH + 1) // 2
N_ODD = DEPTH // 2

kernel_name = 'hybrid_dsa_gdn_retention_trunk'

def _split(x, sizes):
    out, start = [], 0
    for s in sizes:
        out.append(x[..., start:start + s])
        start += s
    return out

def _rms(x):
    xf = x.astype(jnp.float32)
    return xf * lax.rsqrt(jnp.mean(xf * xf, axis=-1, keepdims=True) + NORM_EPS)

def rmsnorm(x, gain):
    return (_rms(x) * gain.astype(jnp.float32)).astype(x.dtype)

def l2norm(x):
    xf = x.astype(jnp.float32)
    return (xf * lax.rsqrt(jnp.sum(xf * xf, axis=-1, keepdims=True) + NORM_EPS)).astype(x.dtype)

def _to_chunks(a):
    front = (-N_META) % CHUNK
    a = jnp.pad(a, [(0, 0), (front, 0)] + [(0, 0)] * (a.ndim - 2))
    b, tp = a.shape[:2]
    a = a.reshape((b, tp // CHUNK, CHUNK) + a.shape[2:])
    return jnp.moveaxis(a, 3, 1)

def _from_chunks(a, t):
    b, h, n, c, d = a.shape
    a = a.reshape(b, h, n * c, d)[:, :, n * c - t:]
    return jnp.moveaxis(a, 1, 2)

def _causal_conv(x, w):
    c = x.shape[-1]
    return lax.conv_general_dilated(
        x, w.reshape(CONV_K, 1, c).astype(x.dtype), window_strides=(1,),
        padding=[(CONV_K - 1, 0)], dimension_numbers=('NWC', 'WIO', 'NWC'),
        feature_group_count=c)

def _rotate_pairs(x, pos):
    d = x.shape[-1]
    inv = 1.0 / (ROT_BASE ** jnp.linspace(0.0, 1.0, d // 2, dtype=jnp.float32))
    ang = pos.astype(jnp.float32)[:, None] * inv[None, :]
    cos, sin = jnp.cos(ang)[:, None, :], jnp.sin(ang)[:, None, :]
    x1 = x[..., 0::2].astype(jnp.float32)
    x2 = x[..., 1::2].astype(jnp.float32)
    y = jnp.stack([x1 * cos - x2 * sin, x1 * sin + x2 * cos], axis=-1)
    return y.reshape(x.shape).astype(x.dtype)

def dsa_attention(c_q, c_kv, k_idx_raw, w_idx_raw, q_norm, w_uq, w_qidx, kv_norm, w_ukv,
                  kidx_norm, n_ctx):
    b, t, _ = c_q.shape
    cq = rmsnorm(c_q, q_norm)
    q = (cq @ w_uq).reshape(b, t, A_HEADS, A_HEAD_DIM)
    q_idx = (cq @ w_qidx).reshape(b, t, IDX_HEADS, IDX_DIM)
    kv = (rmsnorm(c_kv, kv_norm) @ w_ukv).reshape(b, t, A_HEADS, 2 * A_HEAD_DIM)
    k, v = kv[..., :A_HEAD_DIM], kv[..., A_HEAD_DIM:]
    k_idx = rmsnorm(k_idx_raw, kidx_norm).astype(jnp.float32)
    w_idx = w_idx_raw.astype(jnp.float32) * (IDX_HEADS * IDX_DIM) ** -0.5
    top_k = min(TOPK_MAX, n_ctx // TOPK_FRAC)
    scale = A_HEAD_DIM ** -0.5
    n_blk = -(-t // Q_BLOCK)
    pad = n_blk * Q_BLOCK - t
    key_pos = jnp.arange(t)

    def blocks(a):
        a = jnp.pad(a, [(0, 0), (0, pad)] + [(0, 0)] * (a.ndim - 2))
        return jnp.moveaxis(a.reshape((b, n_blk, Q_BLOCK) + a.shape[2:]), 1, 0)

    def one_block(args):
        blk, q_b, qi_b, wi_b = args
        q_pos = blk * Q_BLOCK + jnp.arange(Q_BLOCK)
        causal = key_pos[None, :] <= q_pos[:, None]
        dots = jax.nn.relu(jnp.einsum('bqhd,bsd->bqhs', qi_b.astype(jnp.float32), k_idx))
        score = jnp.einsum('bqh,bqhs->bqs', wi_b, dots)
        score = jnp.where(causal[None], score, -jnp.inf)
        _, sel = lax.top_k(score, top_k)
        valid = sel <= q_pos[None, :, None]
        k_sel = jax.vmap(lambda kk, ii: kk[ii])(k, sel)
        v_sel = jax.vmap(lambda vv, ii: vv[ii])(v, sel)
        logits = jnp.einsum('bqhd,bqkhd->bqhk', q_b, k_sel).astype(jnp.float32) * scale
        logits = jnp.where(valid[:, :, None, :], logits, -jnp.inf)
        p = jax.nn.softmax(logits, axis=-1).astype(v.dtype)
        return jnp.einsum('bqhk,bqkhd->bqhd', p, v_sel)

    out = lax.map(one_block, (jnp.arange(n_blk), blocks(q), blocks(q_idx), blocks(w_idx)))
    out = jnp.moveaxis(out, 0, 1).reshape(b, n_blk * Q_BLOCK, A_WIDTH)
    return out[:, :t]

def _chunk_gated_delta(q, k, v, beta, g):
    f32 = jnp.float32
    t = q.shape[1]
    qc, kc, vc = (_to_chunks(a.astype(f32)) for a in (q, k, v))
    bc = _to_chunks(beta[..., None])[..., 0]
    gcum = jnp.cumsum(_to_chunks(g[..., None])[..., 0], axis=-1)
    lower = jnp.tril(jnp.ones((CHUNK, CHUNK), bool))
    strict = jnp.tril(jnp.ones((CHUNK, CHUNK), bool), -1)
    decay = jnp.exp(jnp.where(lower, gcum[..., :, None] - gcum[..., None, :], -jnp.inf))
    kb = kc * bc[..., None]
    a_mat = jnp.where(strict, jnp.einsum('bhnid,bhnjd->bhnij', kb, kc) * decay, 0.0)
    eye = jnp.eye(CHUNK, dtype=f32)
    t_mat = lax.linalg.triangular_solve(eye + a_mat, jnp.broadcast_to(eye, a_mat.shape),
                                        left_side=True, lower=True, unit_diagonal=True)
    u = t_mat @ (vc * bc[..., None])
    w = t_mat @ (kb * jnp.exp(gcum)[..., None])
    qk = jnp.einsum('bhnid,bhnjd->bhnij', qc, kc) * decay
    qg = qc * jnp.exp(gcum)[..., None]
    kd = kc * jnp.exp(gcum[..., -1:] - gcum)[..., None]
    g_last = jnp.exp(gcum[..., -1])

    def step(state, xs):
        u_i, w_i, qg_i, qk_i, kd_i, gl_i = xs
        v_new = u_i - w_i @ state
        o_i = qg_i @ state + qk_i @ v_new
        state = state * gl_i[..., None, None] + jnp.swapaxes(kd_i, -1, -2) @ v_new
        return state, o_i

    b, h = qc.shape[:2]
    state0 = jnp.zeros((b, h, B_HEAD_DIM, B_HEAD_DIM), f32)
    xs = tuple(jnp.moveaxis(a, 2, 0) for a in (u, w, qg, qk, kd, g_last))
    _, o = lax.scan(step, state0, xs)
    return _from_chunks(jnp.moveaxis(o, 0, 2), t)

def gated_deltanet(qkv, z, beta_raw, a_raw, conv_w, a_log, dt_bias, o_norm):
    b, t, _ = qkv.shape
    f32 = jnp.float32
    qkv = jax.nn.silu(_causal_conv(qkv, conv_w))
    q, k, v = _split(qkv, (B_WIDTH, B_WIDTH, B_WIDTH))
    shp = (b, t, B_HEADS, B_HEAD_DIM)
    q = l2norm(q.reshape(shp)) * B_HEAD_DIM ** -0.5
    k = l2norm(k.reshape(shp))
    v = v.reshape(shp)
    beta = jax.nn.sigmoid(beta_raw.astype(f32))
    g = -jnp.exp(a_log.astype(f32)) * jax.nn.softplus(a_raw.astype(f32) + dt_bias.astype(f32))
    o = _chunk_gated_delta(q, k, v, beta, g)
    o = rmsnorm(o, o_norm) * jax.nn.silu(z.reshape(shp).astype(f32))
    return o.reshape(b, t, B_WIDTH).astype(qkv.dtype)

def _chunk_retention(q, k, v):
    f32 = jnp.float32
    t = q.shape[1]
    qc, kc, vc = (_to_chunks(a.astype(f32)) for a in (q, k, v))
    log_gamma = jnp.log(1.0 - 2.0 ** (-5.0 - jnp.arange(C_HEADS, dtype=f32)))
    pos = jnp.arange(CHUNK, dtype=f32)
    rel = pos[:, None] - pos[None, :]
    dmask = jnp.where(rel >= 0, jnp.exp(jnp.maximum(rel, 0.0)[None] * log_gamma[:, None, None]), 0.0)
    scores = jnp.einsum('bhnid,bhnjd->bhnij', qc, kc) * dmask[None, :, None]
    o_intra = scores @ vc
    q_decay = jnp.exp((pos + 1.0)[None, :] * log_gamma[:, None])
    k_decay = jnp.exp((CHUNK - 1.0 - pos)[None, :] * log_gamma[:, None])
    chunk_decay = jnp.exp(CHUNK * log_gamma)
    qd = qc * q_decay[None, :, None, :, None]
    kd = kc * k_decay[None, :, None, :, None]

    def step(r, xs):
        qd_i, kd_i, v_i = xs
        o_i = qd_i @ r
        r = r * chunk_decay[None, :, None, None] + jnp.swapaxes(kd_i, -1, -2) @ v_i
        return r, o_i

    b, h = qc.shape[:2]
    r0 = jnp.zeros((b, h, C_QK_DIM, C_V_DIM), f32)
    _, o_inter = lax.scan(step, r0, tuple(jnp.moveaxis(a, 2, 0) for a in (qd, kd, vc)))
    return _from_chunks(o_intra + jnp.moveaxis(o_inter, 0, 2), t)

def hybrid_mixer(h, w_in, q_norm, w_uq, w_qidx, kv_norm, w_ukv, kidx_norm,
                 conv_w, a_log, dt_bias, o_norm, w_out, n_ctx):
    c_q, c_kv, k_idx, w_idx, qkv, z, beta_raw, a_raw = _split(h @ w_in, HY_IN_SIZES)
    o_a = dsa_attention(c_q, c_kv, k_idx, w_idx, q_norm, w_uq, w_qidx, kv_norm, w_ukv,
                        kidx_norm, n_ctx)
    o_b = gated_deltanet(qkv, z, beta_raw, a_raw, conv_w, a_log, dt_bias, o_norm)
    return jnp.concatenate([o_a, o_b], axis=-1) @ w_out

def retention_mixer(h, w_in, w_out):
    b, t, _ = h.shape
    q, k, v, gate = _split(h @ w_in, RET_IN_SIZES)
    pos = jnp.arange(t)
    q = _rotate_pairs(q.reshape(b, t, C_HEADS, C_QK_DIM), pos)
    k = _rotate_pairs(k.reshape(b, t, C_HEADS, C_QK_DIM), pos) * C_QK_DIM ** -0.5
    o = _chunk_retention(q, k, v.reshape(b, t, C_HEADS, C_V_DIM))
    o = _rms(o).astype(h.dtype).reshape(b, t, C_V_WIDTH)
    return (jax.nn.silu(gate) * o) @ w_out

def swiglu(h, w_gate, w_up, w_down):
    return (jax.nn.silu(h @ w_gate) * (h @ w_up)) @ w_down

def setup_inputs(seed: int = 0) -> dict:
    key = jax.random.key(seed)
    keys = iter(jax.random.split(key, 32))
    f32 = jnp.float32

    def normal(shape, scale):
        return jax.random.normal(next(keys), shape, f32) * scale

    def gain(shape):
        return 1.0 + normal(shape, 0.02)

    ne, no = N_EVEN, N_ODD
    a_log = jnp.log(jax.random.uniform(next(keys), (ne, B_HEADS), f32, 1.0, 16.0))
    dt = jnp.exp(jax.random.uniform(next(keys), (ne, B_HEADS), f32,
                                    math.log(1e-3), math.log(1e-1)))
    return {
        'x': normal((BATCH, SEQ, D_MODEL), 1.0),
        'meta_tokens': normal((N_META, D_MODEL), 1.0),
        'mix_norm_pre': gain((DEPTH, D_MODEL)),
        'mix_norm_post': gain((DEPTH, D_MODEL)),
        'ffn_norm_pre': gain((DEPTH, D_MODEL)),
        'ffn_norm_post': gain((DEPTH, D_MODEL)),
        'hy_w_in': normal((ne, D_MODEL, HY_IN_COLS), D_MODEL ** -0.5),
        'dsa_q_norm': gain((ne, A_Q_RANK)),
        'dsa_w_uq': normal((ne, A_Q_RANK, A_WIDTH), A_Q_RANK ** -0.5),
        'dsa_w_qidx': normal((ne, A_Q_RANK, IDX_HEADS * IDX_DIM), A_Q_RANK ** -0.5),
        'dsa_kv_norm': gain((ne, A_KV_RANK)),
        'dsa_w_ukv': normal((ne, A_KV_RANK, 2 * A_WIDTH), A_KV_RANK ** -0.5),
        'dsa_kidx_norm': gain((ne, IDX_DIM)),
        'gdn_conv_w': normal((ne, CONV_K, 3 * B_WIDTH), CONV_K ** -0.5),
        'gdn_a_log': a_log,
        'gdn_dt_bias': dt + jnp.log(-jnp.expm1(-dt)),
        'gdn_o_norm': gain((ne, B_HEAD_DIM)),
        'hy_w_out': normal((ne, A_WIDTH + B_WIDTH, D_MODEL), (A_WIDTH + B_WIDTH) ** -0.5),
        'ret_w_in': normal((no, D_MODEL, RET_IN_COLS), D_MODEL ** -0.5),
        'ret_w_out': normal((no, C_V_WIDTH, D_MODEL), C_V_WIDTH ** -0.5),
        'ffn_w_gate': normal((DEPTH, D_MODEL, D_FF), D_MODEL ** -0.5),
        'ffn_w_up': normal((DEPTH, D_MODEL, D_FF), D_MODEL ** -0.5),
        'ffn_w_down': normal((DEPTH, D_FF, D_MODEL), D_FF ** -0.5),
    }

def reference(x, meta_tokens, mix_norm_pre, mix_norm_post, ffn_norm_pre, ffn_norm_post,
              hy_w_in, dsa_q_norm, dsa_w_uq, dsa_w_qidx, dsa_kv_norm, dsa_w_ukv, dsa_kidx_norm,
              gdn_conv_w, gdn_a_log, gdn_dt_bias, gdn_o_norm, hy_w_out,
              ret_w_in, ret_w_out, ffn_w_gate, ffn_w_up, ffn_w_down):
    b, seq, _ = x.shape
    meta = jnp.broadcast_to(meta_tokens[None].astype(x.dtype), (b, N_META, D_MODEL))
    h = jnp.concatenate([meta, x], axis=1)
    for layer in range(DEPTH):
        i = layer // 2
        u = rmsnorm(h, mix_norm_pre[layer])
        if layer % 2 == 0:
            u = hybrid_mixer(u, hy_w_in[i], dsa_q_norm[i], dsa_w_uq[i], dsa_w_qidx[i],
                             dsa_kv_norm[i], dsa_w_ukv[i], dsa_kidx_norm[i], gdn_conv_w[i],
                             gdn_a_log[i], gdn_dt_bias[i], gdn_o_norm[i], hy_w_out[i], seq)
        else:
            u = retention_mixer(u, ret_w_in[i], ret_w_out[i])
        h = h + rmsnorm(u, mix_norm_post[layer])
        u = swiglu(rmsnorm(h, ffn_norm_pre[layer]), ffn_w_gate[layer], ffn_w_up[layer],
                   ffn_w_down[layer])
        h = h + rmsnorm(u, ffn_norm_post[layer])
    return h[:, N_META:]


_drawn_inputs = setup_inputs


def setup_inputs(seed=0):
    import zlib

    import numpy as np

    out = dict(_drawn_inputs(seed))
    spreads = {}
    factors = {'ffn_norm_post': 2.968, 'dsa_kv_norm': 4.69, 'gdn_o_norm': 8.0}
    for name, (base, spread) in spreads.items():
        noise = np.random.default_rng([zlib.crc32(name.encode()), seed]).standard_normal(out[name].shape)
        drawn = base * np.exp(spread * noise) if base else spread * noise
        out[name] = jnp.asarray(drawn.astype(out[name].dtype))
    for name, factor in factors.items():
        out[name] = (out[name] * factor).astype(out[name].dtype)
    return out
```

```python
import math
from contextlib import ExitStack

import numpy as np
import concourse.bass as bass
from concourse import mybir

F32 = mybir.dt.float32
F32R = mybir.dt.float32r
ACT = mybir.ActivationFunctionType
ALU = mybir.AluOpType
AX = mybir.AxisListType

P = 128
D = 2048
META = 16
SEQ = 256
T = META + SEQ
KC = D // P
DFF = 5632
HEADS = 8
EPS = 1e-6
BLK = [(0, 128), (128, 128), (256, 16)]
ROW = [(0, 128), (128, 256), (384, 272)]
ROWS_W = 656
TOPK = 64
IDX_HEADS = 16
IDX_DIM = 64
CH = 91
NCH = 3
LP = CH * NCH
LEVELS = 7
HALF = DFF // P // 2
SUB = HALF // 2
TROW = [(0, 0, 272), (272, 128, 144), (416, 256, 16)]
RROW = [(0, 0, 256), (256, 112, 144), (400, 240, 16)]
MASKED = -1.0e30
NONCAUSAL = -3.0e38
TAKEN = -3.4e38
TAKEN_EDGE = -3.3e38


def stage_table():
    table, at = {}, [0, 0, 0]
    for name, *sizes in (
            ("latent", 8, 8, 8), ("index_q", 2, 8, 8), ("heads", 6 * HEADS, 7 * HEADS, 6 * HEADS),
            ("mix_out", 16, 16, 16),
            ("up0", 2 * HALF, 2 * HALF, 2 * HALF), ("down0", 32, 32, 16),
            ("up1", 2 * HALF, 2 * HALF, 2 * HALF), ("down1", 32, 32, 16),
            ("ret_in", 12 * HEADS, 12 * HEADS, 12 * HEADS), ("ret_out", 32, 32, 16),
            ("up2", 2 * HALF, 2 * HALF, 2 * HALF), ("down2", 32, 32, 16),
            ("up3", 2 * HALF, 2 * HALF, 2 * HALF), ("down3", 32, 32, 16), ("end", 0, 0, 0)):
        table[name] = tuple(at)
        at = [x + y for x, y in zip(at, sizes)]
    return table


class Steps:

    def __init__(self, sem, names):
        self.sem, self.names = sem, names.split()

    def after(self, name, rnd=0):
        return rnd * len(self.names) + (self.names.index(name) + 1)


def trunk(nc, a, out):
    ctx = ExitStack()
    st = stage_table()
    with ctx:
        def sb(name, shape, dt=F32, c=ctx):
            return c.enter_context(nc.sbuf_tensor(name, shape, dt))

        def sem(name):
            return ctx.enter_context(nc.semaphore(name))

        h = sb("h", [P, KC, T])
        x_hi = sb("x_hi", [P, KC, T], F32R)
        x_lo = sb("x_lo", [P, KC, T], F32R)
        u = sb("u", [P, KC, T])
        raw = sb("raw", [P, 2, 16 * P])
        w_hi = sb("w_hi", [P, 2, 16 * P], F32R)
        w_lo = sb("w_lo", [P, 2, 16 * P], F32R)
        gains = sb("gains", [P, 8, KC])
        ones = sb("ones", [P, P])
        ident = sb("ident", [P, P])
        sq = sb("sq", [P, 2, T])
        r_pre = sb("r_pre", [P, T])
        r_post = sb("r_post", [P, T])
        root = sb("root", [P, T])
        eps_col = sb("eps_col", [P, 2])
        flat = u[:, :, :].rearrange("p c t -> p (c t)")
        with ExitStack() as first:
            y_hi = sb("y_hi", [P, KC, T], F32R, first)
            y_lo = sb("y_lo", [P, KC, T], F32R, first)
            cq_hi = sb("cq_hi", [P, 4, T], F32R, first)
            cq_lo = sb("cq_lo", [P, 4, T], F32R, first)
            ckv_hi = sb("ckv_hi", [P, 2, 3 * P], F32R, first)
            ckv_lo = sb("ckv_lo", [P, 2, 3 * P], F32R, first)
            kidx = sb("kidx", [P, T], F32, first)
            bias = sb("bias", [P, ROWS_W], F32, first)
            lat_gain = sb("lat_gain", [P, 8], F32, first)
            widx = sb("widx", [P, 3, IDX_HEADS], F32, first)
            levels = sb("levels", [CH, LEVELS, CH], F32, first)
            upto = sb("upto", [CH, CH], F32, first)
            conv_w = sb("conv_w", [P, HEADS, 3, 4], F32, first)
            gb8 = sb("gb8", [HEADS, 2, LP], F32, first)
            gsel = sb("gsel", [HEADS, 2, LP], F32, first)
            decay8 = sb("decay8", [HEADS, 4], F32, first)
            cols = sb("cols", [CH, 4, NCH, HEADS], F32, first)
            conv_in = sb("conv_in", [P, 3, 3 + T], F32, first)
            conv_acc = sb("conv_acc", [P, 3, T], F32, first)
            qkv = sb("qkv", [P, 3, LP], F32, first)
            gate = sb("gate", [P, T], F32, first)
            kq = sb("kq", [P, 4, LP], F32, first)
            dec = sb("dec", [P, LP], F32, first)
            state = sb("state", [P, P], F32, first)
            v_new = sb("v_new", [CH, NCH, P], F32, first)
            kd_last = sb("kd_last", [CH, NCH], F32, first)
            top8 = sb("top8", [P, 8], F32, first)
            mx = sb("mx", [P, 3], F32, first)
            rs = sb("rs", [P, 3], F32, first)
            rinv = sb("rinv", [P, 3], F32, first)
            v_h = sb("v_h", [P, 3, P], F32, first)
            dsa_s = sb("dsa_s", [P, ROWS_W], F32, first)
            p_t = sb("p_t", [P, 432], F32, first)
        with ExitStack() as second:
            mid_hi = sb("mid_hi", [P, 32 * SEQ], F32R, second)
            mid_lo = sb("mid_lo", [P, 32 * SEQ], F32R, second)
            ffn_g = sb("ffn_g", [P, 2, T], F32, second)
            ffn_m = sb("ffn_m", [P, 2, T], F32, second)
            rope = sb("rope", [P, 2, T], F32, second)
            lg = sb("lg", [P, HEADS], F32, second)
            q_rot = sb("q_rot", [P, 2, SEQ], F32, second)
            k_rot = sb("k_rot", [P, 2, T], F32, second)
            rot_a = sb("rot_a", [P, 2, T], F32, second)
            ret_sq = sb("ret_sq", [P, 4, SEQ], F32, second)
            ret_r = sb("ret_r", [P, SEQ], F32, second)

        def carve(cursor, shape):
            n = int(np.prod(shape[1:]))
            part = flat[0:shape[0], cursor[0]:cursor[0] + n]
            cursor[0] += n
            assert cursor[0] <= KC * T
            return part if len(shape) == 2 else part.rearrange("p (x y) -> p x y", x=shape[1])

        c1 = [0]
        lat = carve(c1, [P, 8, T])
        q_index = carve(c1, [P, 8, T])
        c2 = [0]
        at = carve(c2, [CH, NCH, CH])
        at_l = carve(c2, [CH, NCH, CH])
        qk = carve(c2, [CH, NCH, CH])
        tm = carve(c2, [CH, NCH, CH])
        tt = carve(c2, [CH, NCH, CH])
        ym = carve(c2, [CH, NCH, CH])
        kbg = carve(c2, [CH, NCH, P])
        kd = carve(c2, [CH, NCH, P])
        vb = carve(c2, [CH, NCH, P])
        wneg = carve(c2, [P, LP])
        c3 = list(c2)
        q_h = carve(c3, [P, T])
        k_h = carve(c3, [P, T])
        c4 = [0]
        rel = carve(c4, [P, 416])
        dmask = carve(c4, [P, 416])
        ret_s = carve(c4, [P, 416])
        v_rows = carve(c4, [P, 3, 512])
        v_t = carve(c4, [P, T])
        ret_g = carve(c4, [P, 4, SEQ])

        ps = ctx.enter_context(nc.psum_tensor("ps", [P, 8, 512], F32))
        BK_SUM, BK_D0, BK_D1, BK_0, BK_1, BK_2, BK_3 = 2, 2, 3, 4, 5, 6, 7

        h_in = [sem(f"h_in{i}") for i in range(4)]
        const_in = sem("const_in")
        rel_in = sem("rel_in")
        const1_in = sem("const1_in")
        piece_in = [sem("piece_in0"), sem("piece_in1")]
        hi_ready = sem("hi_ready")
        lo_ready = sem("lo_ready")
        products = sem("products")
        drained = sem("drained")
        scaled = sem("scaled")
        h_ready = sem("h_ready")
        x_hi_ready = sem("x_hi_ready")
        x_lo_ready = sem("x_lo_ready")
        squared = sem("squared")
        summed = sem("summed")
        rooted = sem("rooted")
        r_ready = sem("r_ready")
        gate_silu = sem("gate_silu")
        mid_ready = sem("mid_ready")
        mid_hi_ready = sem("mid_hi_ready")
        mid_lo_ready = sem("mid_lo_ready")
        out_done = sem("out_done")

        LA = Steps(sem("lat_act"), "squared rooted hi_q hi_kv beta_exp exp ln a_exp decayed")
        LP_ = Steps(sem("lat_pe"), "summed index_w columns")
        LV = Steps(sem("lat_dve"), "recip norm_q norm_kv lo shifted dt max abs one packed softplus nea decay "
                   "scan0 scan1 scan2 widx cols01 cols3")
        dots = sem("dots")
        relued = sem("relued")
        scored = sem("scored")
        TV = Steps(sem("top_dve"), " ".join(f"m{i} r{i}" for i in range(TOPK // 8)) + " chosen")
        TG = Steps(sem("top_pool"), "causal final")

        CV = Steps(sem("conv_dve"), "t00 t01 t02 t03 t10 t11 t12 t13 t20 t21 t22 t23")
        CA = Steps(sem("conv_act"), "silu0 silu1 silu2 gate")

        DP = Steps(sem("dsa_pe"), "logits turned attended")
        DV = Steps(sem("dsa_dve"), "inputs scored maxed recips probs y_lo")
        DA = Steps(sem("dsa_act"), "exped turned y_hi")

        GP = Steps(sem("gdn_pe"), "sums spread scores turned tm0 "
                   + " ".join(f"y{i} z{i}" for i in range(1, LEVELS)) + " w v0 o0 v1 o1 v2 o2 osum")
        GA = Steps(sem("gdn_act"), "squared ln rnorm decayed decmat "
                   + " ".join(f"y{i}" for i in range(1, LEVELS)) + " w osq oln ornorm y_hi")
        GV = Steps(sem("gdn_dve"), "select kq kb arg masked mats rows at0 tt0 tm0 "
                   + " ".join(f"tm{i} tt{i}" for i in range(1, LEVELS - 1)) + f" tt{LEVELS - 1}"
                   + " vn0 s0 vn1 s1 vn2 om0 om1 y_lo")
        GG = Steps(sem("gdn_pool"), " ".join(f"lev{i}" for i in range(1, LEVELS)))

        RP = Steps(sem("ret_pe"), "vt0 vt1 vt2 vt3 scores o osum")
        RV = Steps(sem("ret_dve"), "s s2 recip gr y y_lo")
        RA = Steps(sem("ret_act"), "dmask vr0 vr1 vr2 vr3 g0 g1 osq g2 rooted g3 y_hi")
        RG = Steps(sem("ret_pool"), "q k")
        rope_ready = sem("rope_ready")

        cleared = sem("cleared")
        block = ctx.enter_context(nc.Block())

        def ds1(i):
            return bass.ds(i, 1)

        def rounds(eng, n, body):
            if n > 1:
                with eng.Fori(0, n - 1) as i:
                    body(i, False)
            body(n - 1, True)

        FFN_W = SUB * P
        FULL = 16 * P
        HEAD_W = [FULL, FULL, FULL, FULL, 4 * P, 4 * P]

        @block.sync
        def _(sp):
            for i in range(4):
                sp.dma_start(h[:, 4 * i:4 * i + 4, :], a["x_t"][:, 4 * i:4 * i + 4, :]).then_inc(h_in[i], 16)
                if i == 0:
                    sp.dma_start(gains[:], a["gains"]).then_inc(const_in, 16)
                if i == 1:
                    sp.dma_start(raw[:, 0], a["w_latent"][0]).then_inc(piece_in[0], 16)
            sp.dma_start(raw[:, 1], a["w_latent"][1]).then_inc(piece_in[1], 16)
            sp.dma_start(ones[:], a["ones"]).then_inc(const_in, 16)
            sp.dma_start(ident[:], a["ident"]).then_inc(const_in, 16)
            sp.dma_start(lat_gain[:, :], a["lat_gain"]).then_inc(const_in, 16)
            sp.dma_start(levels[:], a["levels"]).then_inc(const_in, 16)
            sp.dma_start(upto[:], a["upto"]).then_inc(const_in, 16)
            sp.dma_start(conv_w[:], a["conv_w"]).then_inc(const_in, 16)
            sp.dma_start(decay8[:, 0:2], a["decay8"]).then_inc(const_in, 16)

            def load(slot, width, src, piece):
                sp.wait_ge(lo_ready, piece - 1)
                sp.dma_start(raw[:, slot, 0:width], src).then_inc(piece_in[slot], 16)

            base = st["latent"][0]
            with sp.Fori(1, 4) as i:
                for s in range(2):
                    load(s, FULL, a["w_latent"][ds1(2 * i + s)], base + 2 * i + s)
            base = st["index_q"][0]
            for s in range(2):
                load(s, FULL, a["w_index_q"][s], base + s)
            base = st["heads"][0]
            with sp.Fori(0, HEADS) as i:
                for s in range(4):
                    load(s % 2, FULL, a["w_heads"][ds1(4 * i + s)], base + 6 * i + s)
                for s in range(2):
                    load(s, 4 * P, a["w_dsa"][ds1(2 * i + s)], base + 6 * i + 4 + s)
            base = st["mix_out"][0]
            with sp.Fori(0, 8) as i:
                for s in range(2):
                    load(s, FULL, a["w_mix_out"][ds1(2 * i + s)], base + 2 * i + s)

            def ffn(layer):
                for half in range(2):
                    n = 2 * layer + half
                    base = st[f"up{n}"][0]
                    with sp.Fori(0, HALF) as i:
                        for s in range(2):
                            load(s, FULL, a["w_up"][ds1(2 * HALF * n + 2 * i + s)], base + 2 * i + s)
                    base = st[f"down{n}"][0]
                    with sp.Fori(0, KC) as i:
                        for s in range(2):
                            load(s, FFN_W, a["w_down"][ds1(2 * KC * n + 2 * i + s)], base + 2 * i + s)

            ffn(0)
            sp.wait_ge(products, st["mix_out"][1] + 16)
            sp.dma_start(rope[:], a["rope"]).then_inc(const1_in, 16)
            sp.dma_start(lg[:], a["log_gamma"]).then_inc(const1_in, 16)
            base = st["ret_in"][0]
            with sp.Fori(0, 6 * HEADS) as i:
                for s in range(2):
                    load(s, FULL, a["w_ret_in"][ds1(2 * i + s)], base + 2 * i + s)
            base = st["ret_out"][0]
            with sp.Fori(0, KC) as i:
                for s in range(2):
                    load(s, FULL, a["w_ret_out"][ds1(2 * i + s)], base + 2 * i + s)
            ffn(1)
            for i in range(4):
                sp.wait_ge(h_ready, 3 * KC + 4 * i + 4)
                sp.dma_start(out[:, 4 * i:4 * i + 4, :], h[:, 4 * i:4 * i + 4, META:T]).then_inc(out_done, 16)
            sp.wait_ge(out_done, 4 * 16)

        CONSTS0 = 8 * 16
        CONSTS1 = 2 * 16

        FROM = [0, 0, 0, 0, 0, META, META, META]

        @block.tensor
        def _(pe):
            def mm(o, lhs, rhs, start, stop):
                return nc.tensor.matmul(o, lhs, rhs, start=start, stop=stop)

            def multiply(o, slot, w0, n, xh, xl, start=True, stop=True, before=None, behind=None):
                for k in range(n):
                    wh = w_hi[:, slot, (w0 + k) * P:(w0 + k + 1) * P]
                    wl = w_lo[:, slot, (w0 + k) * P:(w0 + k + 1) * P]
                    if before:
                        before(k)
                    mm(o, wh, xh(k), start and k == 0, False)
                    mm(o, wh, xl(k), False, False)
                    last = mm(o, wl, xh(k), False, stop and k == n - 1)
                    if behind:
                        behind(k)
                return last

            def open_tile(piece, tile):
                pe.wait_ge(lo_ready, piece + 1)
                if not (isinstance(tile, int) and tile < 2):
                    pe.wait_ge(drained, tile - 1)

            def sum_of(norm, k, slot):
                t0 = FROM[norm]
                pe.wait_ge(squared, KC * norm + k + 1)
                first = isinstance(k, int) and k == 0
                if first and norm:
                    pe.wait_ge(rooted, norm)
                mm(ps[:, BK_SUM, t0:T], ones[:], sq[:, slot, t0:T], first,
                   isinstance(k, int) and k == KC - 1).then_inc(summed, 1)

            def from_x(stage, n_pairs, norm=None, t0=0):
                base, _, tile0 = st[stage]

                def xh(k):
                    return x_hi[:, k, t0:T]

                def xl(k):
                    return x_lo[:, k, t0:T]

                for s in range(2):
                    open_tile(base + s, tile0 + s)
                    fresh = norm is not None and s == 0
                    last = multiply(ps[:, s, t0:T], s, 0, KC, xh, xl,
                                    before=(lambda k: pe.wait_ge(x_lo_ready, KC * (norm // 2) + k + 1))
                                    if fresh else None,
                                    behind=(lambda k: sum_of(norm, k, k % 2)) if fresh else None)
                    last.then_inc(products, 1)
                with pe.Fori(1, n_pairs) as i:
                    for s in range(2):
                        open_tile(base + 2 * i + s, tile0 + 2 * i + s)
                        multiply(ps[:, s, t0:T], s, 0, KC, xh, xl).then_inc(products, 1)

            def out_proj(stage, n_sub, n_chunks, width, src_hi, src_lo, t0, norm, ready):
                base, _, tile0 = st[stage]

                def tile(i, s, fresh):
                    for sub in range(n_sub):
                        slot = (n_sub * s + sub) % 2
                        if sub == 0:
                            open_tile(base + n_sub * (2 * i + s), tile0 + 2 * i + s)
                        else:
                            pe.wait_ge(lo_ready, base + n_sub * (2 * i + s) + sub + 1)
                        multiply(ps[:, s, t0:T], slot, 0, n_chunks,
                                 lambda k: src_hi(sub * n_chunks + k), lambda k: src_lo(sub * n_chunks + k),
                                 sub == 0, sub == n_sub - 1,
                                 before=(lambda k: ready(sub * n_chunks + k)) if fresh else None
                                 ).then_inc(products, 1)

                for s in range(2):
                    tile(0, s, s == 0)
                    if norm is not None and s:
                        sum_of(norm, 0, 0)
                with pe.Fori(1, 8) as i:
                    for s in range(2):
                        tile(i, s, False)
                        if norm is not None:
                            sum_of(norm, 2 * i + s - 1, (s + 1) % 2)
                if norm is not None:
                    sum_of(norm, KC - 1, 1)

            pe.wait_ge(const_in, CONSTS0)
            pe.wait_ge(cleared, 1)
            from_x("latent", 4, norm=0)
            pe.wait_ge(LA.sem, LA.after("squared"))
            pe.wait_ge(rooted, 1)
            for k in range(4):
                mm(ps[:, BK_D0, 0:T], ones[:], q_index[:, k], k == 0, k == 3)
            for k in range(2):
                mm(ps[:, BK_D1, 0:T], ones[:], q_index[:, 4 + k], k == 0, k == 1)
            mm(ps[:, BK_0, 0:T], ones[:], q_index[:, 6], True, True).then_inc(LP_.sem, 1)
            for b, (q0, n) in enumerate(BLK):
                last = nc.tensor.transpose(ps[0:n, BK_1, 16 * b:16 * b + 16], lat[0:16, 7, q0:q0 + n],
                                           ident[0:16, 0:16])
            last.then_inc(LP_.sem, 1)
            pe.wait_ge(LV.sem, LV.after("scan2"))
            for w in range(2):
                for n in range(NCH):
                    c = (w * NCH + n) * HEADS
                    last = nc.tensor.transpose(ps[0:CH, BK_2, c:c + HEADS], gb8[:, w, n * CH:(n + 1) * CH],
                                               ident[0:HEADS, 0:HEADS])
            last.then_inc(LP_.sem, 1)

            base, _, tile0 = st["index_q"]
            pe.wait_ge(LV.sem, LV.after("lo"))
            for t in range(8):
                open_tile(base + t // 4, tile0 + t)
                multiply(ps[:, t % 2, 0:T], t // 4, 4 * (t % 4), 4, lambda k: cq_hi[:, k], lambda k: cq_lo[:, k]
                         ).then_inc(products, 1)

            def index_block(b):
                q0, n = BLK[b]
                keys = ROW[b][1]
                for i in range(IDX_HEADS):
                    c = IDX_HEADS * b + i
                    half = IDX_DIM * (i % 2)
                    if c >= 2:
                        pe.wait_ge(relued, c - 1)
                    mm(ps[0:n, BK_D0 + c % 2, 0:keys], q_index[half:half + IDX_DIM, i // 2, q0:q0 + n],
                       kidx[half:half + IDX_DIM, 0:keys], True, True).then_inc(dots, 1)

            pe.wait_ge(drained, st["index_q"][2] + 8)
            for b in range(3):
                index_block(b)

            def head_tiles(i):
                base, _, tile0 = st["heads"]
                for s in range(4):
                    open_tile(base + 6 * i + s, tile0 + 6 * i + s)
                    multiply(ps[:, s % 2, 0:T], s % 2, 0, KC, lambda k: x_hi[:, k], lambda k: x_lo[:, k]
                             ).then_inc(products, 1)
                open_tile(base + 6 * i + 4, tile0 + 6 * i + 4)
                multiply(ps[:, 0, 0:T], 0, 0, 4, lambda k: cq_hi[:, k], lambda k: cq_lo[:, k]).then_inc(products, 1)
                open_tile(base + 6 * i + 5, tile0 + 6 * i + 5)
                multiply(ps[:, 1, 0:T], 1, 0, 2, lambda k: ckv_hi[:, k, 0:T], lambda k: ckv_lo[:, k, 0:T]
                         ).then_inc(products, 1)
                for b in range(3):
                    o = ps[:, BK_D0, b * P:(b + 1) * P]
                    for k in range(2):
                        xh, xl = ckv_hi[:, k, b * P:(b + 1) * P], ckv_lo[:, k, b * P:(b + 1) * P]
                        wh, wl = w_hi[:, 1, (2 + k) * P:(3 + k) * P], w_lo[:, 1, (2 + k) * P:(3 + k) * P]
                        mm(o, xh, wh, k == 0, False)
                        mm(o, xl, wh, False, False)
                        last = mm(o, xh, wl, False, k == 1)
                last.then_inc(products, 1)

            def attend(i):
                pe.wait_ge(DV.sem, DV.after("inputs", i))
                for b, (q0, n) in enumerate(BLK):
                    keys = ROW[b][1]
                    o = ps[0:n, BK_D0, 128 * b:128 * b + keys] if b < 2 else ps[0:n, BK_D1, 0:keys]
                    last = mm(o, q_h[:, q0:q0 + n], k_h[:, 0:keys], True, True)
                last.then_inc(DP.sem, 1)
                pe.wait_ge(DV.sem, DV.after("probs", i))
                for kb, (c0, qf, nq) in enumerate(TROW):
                    k0, nk = BLK[kb]
                    for b, (q0, n) in enumerate(BLK):
                        if b >= kb:
                            c = c0 + q0 - qf
                            last = nc.tensor.transpose(ps[0:nk, BK_D0, c:c + n],
                                                       dsa_s[0:n, ROW[b][0] + k0:ROW[b][0] + k0 + nk],
                                                       ident[0:n, 0:n])
                last.then_inc(DP.sem, 1)
                pe.wait_ge(DA.sem, DA.after("turned", i))
                for kb, (c0, qf, nq) in enumerate(TROW):
                    nk = BLK[kb][1]
                    last = mm(ps[:, BK_D1, qf:qf + nq], v_h[0:nk, kb, :], p_t[0:nk, c0:c0 + nq], kb == 0, kb == 2)
                last.then_inc(DP.sem, 1)

            def delta(i):
                def c(n):
                    return slice(n * CH, (n + 1) * CH)

                pe.wait_ge(GA.sem, GA.after("squared", i))
                mm(ps[:, BK_0, 0:T], ones[:], kq[:, 2, 0:T], True, True)
                mm(ps[:, BK_1, 0:T], ones[:], kq[:, 3, 0:T], True, True).then_inc(GP.sem, 1)
                pe.wait_ge(GV.sem, GV.after("select", i))
                mm(ps[:, BK_2, 0:LP], ones[0:HEADS, :], gsel[:, 0, :], True, True)
                mm(ps[:, BK_3, 0:LP], ones[0:HEADS, :], gsel[:, 1, :], True, True).then_inc(GP.sem, 1)
                pe.wait_ge(GV.sem, GV.after("kb", i))
                for n in range(NCH):
                    mm(ps[0:CH, BK_0, c(n)], kq[:, 0, c(n)], kq[:, 2, c(n)], True, True)
                for n in range(NCH):
                    last = mm(ps[0:CH, BK_1, c(n)], kq[:, 0, c(n)], kq[:, 1, c(n)], True, True)
                last.then_inc(GP.sem, 1)
                pe.wait_ge(GV.sem, GV.after("arg", i))
                pe.wait_ge(GA.sem, GA.after("decayed", i))
                for n in range(NCH):
                    nc.tensor.transpose(ps[0:CH, BK_2, n * P:(n + 1) * P], kq[:, 0, c(n)], ident[:])
                for n in range(NCH):
                    last = nc.tensor.transpose(ps[0:CH, BK_3, n * P:(n + 1) * P], qkv[:, 2, c(n)], ident[:])
                last.then_inc(GP.sem, 1)
                pe.wait_ge(GV.sem, GV.after("tt0", i))
                for n in range(NCH):
                    last = nc.tensor.transpose(ps[0:CH, BK_0, c(n)], tt[:, n], ident[0:CH, 0:CH])
                last.then_inc(GP.sem, 1)
                for l in range(1, LEVELS):
                    pe.wait_ge(GG.sem, GG.after(f"lev{l}", i))
                    pe.wait_ge(GV.sem, GV.after("tm0" if l == 1 else f"tt{l - 1}", i))
                    for n in range(NCH):
                        last = mm(ps[0:CH, BK_1, c(n)], at_l[:, n], tm[:, n], True, True)
                    last.then_inc(GP.sem, 1)
                    pe.wait_ge(GA.sem, GA.after(f"y{l}", i))
                    for n in range(NCH):
                        if l < LEVELS - 1:
                            mm(ps[0:CH, BK_0, c(n)], tt[:, n], ym[:, n], True, True)
                    for n in range(NCH):
                        last = mm(ps[0:CH, BK_2, c(n)], ym[:, n], tt[:, n], True, True)
                    last.then_inc(GP.sem, 1)
                pe.wait_ge(GV.sem, GV.after(f"tt{LEVELS - 1}", i))
                for n in range(NCH):
                    last = mm(ps[:, BK_1, c(n)], kbg[:, n], tt[:, n], True, True)
                last.then_inc(GP.sem, 1)
                for n in range(NCH):
                    if n:
                        pe.wait_ge(GV.sem, GV.after(f"s{n - 1}", i))
                    mv = mm(ps[0:CH, BK_3, n * P:(n + 1) * P], tt[:, n], vb[:, n], True, n == 0)
                    if n:
                        if n == 1:
                            pe.wait_ge(GA.sem, GA.after("w", i))
                        mv = mm(ps[0:CH, BK_3, n * P:(n + 1) * P], wneg[:, c(n)], state[:], False, True)
                    mv.then_inc(GP.sem, 1)
                    pe.wait_ge(GV.sem, GV.after(f"vn{n}", i))
                    if n:
                        mm(ps[:, BK_0, c(n)], state[:], kq[:, 3, c(n)], True, False)
                    last = mm(ps[:, BK_0, c(n)], v_new[:, n], qk[:, n], n == 0, True)
                    if n < NCH - 1:
                        last = mm(ps[:, BK_2, 0:P], kd[:, n], v_new[:, n], True, True)
                    last.then_inc(GP.sem, 1)
                pe.wait_ge(GA.sem, GA.after("osq", i))
                mm(ps[:, BK_1, 0:T], ones[:], kq[:, 2, 0:T], True, True).then_inc(GP.sem, 1)

            with pe.Fori(0, HEADS) as i:
                head_tiles(i)
                attend(i)
                delta(i)

            def ready_y(k):
                if k == 0:
                    pe.wait_ge(DV.sem, DV.after("y_lo", HEADS - 1))
                    pe.wait_ge(GV.sem, GV.after("y_lo", HEADS - 1))

            out_proj("mix_out", 1, KC, FULL, lambda k: y_hi[:, k], lambda k: y_lo[:, k], 0, 1, ready_y)

            def ffn(layer, norm):
                t0 = FROM[norm]
                w = T - t0
                for half in range(2):
                    n = 2 * layer + half
                    from_x(f"up{n}", HALF, norm=norm if half == 0 else None, t0=t0)
                    out_proj(f"down{n}", 2, SUB, FFN_W,
                             lambda k: mid_hi[:, k * w:(k + 1) * w], lambda k: mid_lo[:, k * w:(k + 1) * w], t0,
                             norm + 1 if half else None,
                             lambda k: pe.wait_ge(mid_lo_ready, HALF * n + k + 1))

            ffn(0, 2)

            base, _, tile0 = st["ret_in"]

            def ret_tile(i, s, t0=0, norm=None):
                open_tile(base + 12 * i + s, tile0 + 12 * i + s)
                multiply(ps[:, s % 2, t0:T], s % 2, 0, KC, lambda k: x_hi[:, k, t0:T], lambda k: x_lo[:, k, t0:T],
                         before=(lambda k: pe.wait_ge(x_lo_ready, KC * (norm // 2) + k + 1)) if norm else None,
                         behind=(lambda k: sum_of(norm, k, k % 2)) if norm else None).then_inc(products, 1)

            def turn_v(i, j):
                pe.wait_ge(drained, tile0 + 12 * i + 4 + j + 1)
                if j:
                    pe.wait_ge(RA.sem, RA.after(f"vr{j - 1}", i))
                for b, (q0, n) in enumerate(BLK):
                    last = nc.tensor.transpose(ps[0:n, BK_D1, b * P:(b + 1) * P], v_t[:, q0:q0 + n], ident[:])
                last.then_inc(RP.sem, 1)

            def ret_round(i, norm=None):
                for s in range(4):
                    ret_tile(i, s, META if s < 2 else 0, norm if s == 0 else None)
                ret_tile(i, 4)
                ret_tile(i, 5)
                turn_v(i, 0)
                ret_tile(i, 6)
                turn_v(i, 1)
                ret_tile(i, 7)
                turn_v(i, 2)
                ret_tile(i, 8, META)
                turn_v(i, 3)
                pe.wait_ge(RG.sem, RG.after("k", i))
                for kb, (c0, q0, nq) in enumerate(RROW):
                    k0, nk = BLK[kb]
                    for c in range(2):
                        last = mm(ps[0:nk, BK_D0, c0:c0 + nq], k_rot[:, c, k0:k0 + nk], q_rot[:, c, q0:q0 + nq],
                                  c == 0, c == 1)
                last.then_inc(RP.sem, 1)
                ret_tile(i, 9, META)
                pe.wait_ge(RV.sem, RV.after("s2", i))
                pe.wait_ge(RA.sem, RA.after("vr3", i))
                for j in range(4):
                    for kb, (c0, q0, nq) in enumerate(RROW):
                        nk = BLK[kb][1]
                        c = SEQ * (j % 2) + q0
                        last = mm(ps[:, BK_0 + j // 2, c:c + nq], v_rows[0:nk, kb, j * P:(j + 1) * P],
                                  ret_s[0:nk, c0:c0 + nq], kb == 0, kb == 2)
                last.then_inc(RP.sem, 1)
                ret_tile(i, 10, META)
                pe.wait_ge(RA.sem, RA.after("osq", i))
                for j in range(4):
                    last = mm(ps[:, BK_2, 0:SEQ], ones[:], ret_sq[:, j], j == 0, j == 3)
                last.then_inc(RP.sem, 1)
                ret_tile(i, 11, META)

            ret_round(0, 4)
            with pe.Fori(1, HEADS) as i:
                ret_round(i)

            def ready_ret(k):
                if k == 0:
                    pe.wait_ge(RV.sem, RV.after("y_lo", HEADS - 1))

            out_proj("ret_out", 2, KC, FULL, lambda k: mid_hi[:, k * SEQ:(k + 1) * SEQ],
                     lambda k: mid_lo[:, k * SEQ:(k + 1) * SEQ], META, 5, ready_ret)
            ffn(1, 6)

        @block.scalar
        def _(act):
            def split_hi(stage, nth, width, piece, signals):
                act.wait_ge(piece_in[piece % 2], 16 * nth)
                if signals is not None:
                    act.wait_ge(products, signals)
                nc.scalar.activation(w_hi[:, piece % 2, 0:width], raw[:, piece % 2, 0:width],
                                     ACT.Copy).then_inc(hi_ready, 1)

            def split_next(stage, i, q, per_round, width, done=None):
                base, sig, _ = st[stage]
                split_hi(stage, base // 2 + per_round // 2 * i + (q + 1) // 2 + 1, width, q + 1,
                         sig + per_round * i + q if done is None else sig + done)

            def apart():
                act.wait_ge(cleared, 1)

            def square(norm, k, slot, src, src_ready, ready_at):
                t0 = FROM[norm]
                act.wait_ge(src_ready, ready_at)
                n = KC * norm + k
                if not (isinstance(n, int) and n < 2):
                    act.wait_ge(summed, n - 1)
                apart()
                nc.scalar.activation(sq[:, slot, t0:T], src[:, ds1(k), t0:T], ACT.Square).then_inc(squared, 1)

            def take_root(norm):
                t0 = FROM[norm]
                act.wait_ge(summed, KC * (norm + 1))
                if norm:
                    act.wait_ge(r_ready, norm)
                nc.scalar.activation(root[:, t0:T], ps[:, BK_SUM, t0:T], ACT.Sqrt, scale=1.0 / D, bias=eps_col[:, 0:1]
                                     ).then_inc(rooted, 1)

            def fill_x(norm, loaded):
                t0 = FROM[norm]

                def chunk(k, slot):
                    n = KC * norm + k
                    if not loaded:
                        act.wait_ge(h_ready, KC * (norm // 2 - 1) + k + 1)
                    if not (isinstance(n, int) and n < 2):
                        act.wait_ge(summed, n - 1)
                    apart()
                    nc.scalar.activation(x_hi[:, ds1(k), t0:T], h[:, ds1(k), t0:T], ACT.Copy,
                                         scale=gains[:, norm, ds1(k)]).then_inc(x_hi_ready, 1)
                    nc.scalar.activation(sq[:, slot, t0:T], h[:, ds1(k), t0:T], ACT.Square).then_inc(squared, 1)

                if loaded:
                    for k in range(KC):
                        if k % 4 == 0:
                            act.wait_ge(h_in[k // 4], 16)
                        chunk(k, k % 2)
                else:
                    with act.Fori(0, KC // 2) as i:
                        for s in range(2):
                            chunk(2 * i + s, s)
                take_root(norm)

            def plain(stage, n_pairs, next_width):
                def body(i, last):
                    for s in range(2):
                        split_next(stage, i, s, 2, next_width if last and s else FULL)
                rounds(act, n_pairs, body)

            def out_proj(stage, n_sub, width, next_width, norm):
                tile0 = st[stage][2]

                def body(i, last):
                    for s in range(2):
                        for sub in range(n_sub):
                            q = n_sub * s + sub
                            w = next_width if last and q == 2 * n_sub - 1 else width
                            if w:
                                split_next(stage, i, q, 2 * n_sub, w)
                        if norm is not None:
                            square(norm, 2 * i + s, s, u, drained, tile0 + 2 * i + s + 1)
                rounds(act, 8, body)
                if norm is not None:
                    take_root(norm)

            act.wait_ge(const_in, CONSTS0)
            act.wait_ge(cleared, 1)
            split_hi("latent", 1, FULL, 0, None)
            fill_x(0, True)
            split_hi("latent", 1, FULL, 1, None)
            for q in range(1, 8):
                i, s = divmod(q, 2)
                split_next("latent", i, s, 2, FULL)

            act.wait_ge(drained, 8)
            nc.scalar.activation(q_index[:, 0:7], lat[:, 0:7], ACT.Square).then_inc(LA.sem, 1)
            act.wait_ge(LP_.sem, LP_.after("summed"))
            for r, (bank, width) in enumerate(((BK_D0, 4 * P), (BK_D1, 2 * P), (BK_0, P))):
                last = nc.scalar.activation(conv_acc[:, r], ps[:, bank, 0:T], ACT.Sqrt, scale=1.0 / width,
                                            bias=eps_col[:, 0:1])
            last.then_inc(LA.sem, 1)
            act.wait_ge(LV.sem, LV.after("norm_q"))
            nc.scalar.activation(cq_hi[:], lat[:, 0:4], ACT.Copy).then_inc(LA.sem, 1)
            act.wait_ge(LV.sem, LV.after("norm_kv"))
            nc.scalar.activation(ckv_hi[:, :, 0:T], lat[:, 4:6], ACT.Copy).then_inc(LA.sem, 1)
            act.wait_ge(LV.sem, LV.after("shifted"))
            nc.scalar.activation(gb8[:, 1, 0:T], gb8[:, 1, 0:T], ACT.Exp, scale=-1.0).then_inc(LA.sem, 1)
            act.wait_ge(LV.sem, LV.after("abs"))
            nc.scalar.activation(gsel[:, 1, 0:T], gsel[:, 1, 0:T], ACT.Exp).then_inc(LA.sem, 1)
            act.wait_ge(LA.sem, LA.after("exp"))
            nc.scalar.activation(gsel[:, 1, 0:T], gsel[:, 1, 0:T], ACT.Ln, bias=eps_col[0:HEADS, 1:2]).then_inc(LA.sem, 1)
            nc.scalar.activation(decay8[:, 2:3], decay8[:, 0:1], ACT.Exp).then_inc(LA.sem, 1)
            act.wait_ge(LV.sem, LV.after("cols01"))
            nc.scalar.activation(cols[:, 2], cols[:, 0], ACT.Exp).then_inc(LA.sem, 1)

            split_next("index_q", 0, 0, 2, FULL, done=0)
            split_next("index_q", 0, 1, 2, FULL, done=4)
            for b, (q0, n) in enumerate(BLK):
                for i in range(IDX_HEADS):
                    c = IDX_HEADS * b + i
                    act.wait_ge(dots, c + 1)
                    if c >= 2:
                        act.wait_ge(scored, c - 1)
                    nc.scalar.activation(conv_acc[0:n, c % 2, 0:ROW[b][1]], ps[0:n, BK_D0 + c % 2, 0:ROW[b][1]],
                                         ACT.Relu).then_inc(relued, 1)

            def head_tiles(i, last):
                base, sig, tile0 = st["heads"]
                done = [0, 1, 2, 3, 4, 5]
                for s in range(6):
                    split_hi("heads", base // 2 + 3 * i + (s + 1) // 2 + 1,
                             FULL if s in (5, 0, 1, 2) else 4 * P, s + 1, sig + 7 * i + done[s])
                    if s < 3:
                        act.wait_ge(CV.sem, CV.after(f"t{s}3", i))
                        nc.scalar.activation(qkv[:, s, 0:T], conv_acc[:, s], ACT.Silu).then_inc(CA.sem, 1)
                    if s == 3:
                        act.wait_ge(drained, tile0 + 6 * i + 4)
                        nc.scalar.activation(gate[:], gate[:], ACT.Silu).then_inc(CA.sem, 1)

            def attend(i):
                act.wait_ge(DV.sem, DV.after("maxed", i))
                for b, (q0, n) in enumerate(BLK):
                    c0, keys = ROW[b]
                    last = nc.scalar.activation(dsa_s[0:n, c0:c0 + keys], dsa_s[0:n, c0:c0 + keys], ACT.Exp,
                                                bias=mx[0:n, b:b + 1], accum_out=rs[0:n, b:b + 1])
                last.then_inc(DA.sem, 1)
                act.wait_ge(DP.sem, DP.after("turned", i))
                nc.scalar.activation(p_t[:, 0:416], ps[:, BK_D0, 0:416], ACT.Copy)
                nc.scalar.activation(p_t[0:16, 416:432], ps[0:16, BK_D0, 416:432], ACT.Copy).then_inc(DA.sem, 1)
                act.wait_ge(DP.sem, DP.after("attended", i))
                apart()
                nc.scalar.activation(y_hi[:, ds1(i), :], ps[:, BK_D1, 0:T], ACT.Copy).then_inc(DA.sem, 1)

            def delta(i):
                act.wait_ge(CA.sem, CA.after("silu1", i))
                nc.scalar.activation(kq[:, 2:4, 0:T], qkv[:, 0:2, 0:T], ACT.Square).then_inc(GA.sem, 1)
                act.wait_ge(GP.sem, GP.after("sums", i))
                nc.scalar.activation(kq[:, 2:4, 0:T], ps[:, BK_0:BK_1 + 1, 0:T], ACT.Ln, bias=eps_col[:, 0:1]
                                     ).then_inc(GA.sem, 1)
                act.wait_ge(GA.sem, GA.after("ln", i))
                nc.scalar.activation(kq[:, 2:4, 0:T], kq[:, 2:4, 0:T], ACT.Exp, scale=-0.5).then_inc(GA.sem, 1)
                act.wait_ge(GP.sem, GP.after("spread", i))
                nc.scalar.activation(dec[:], ps[:, BK_2, 0:LP], ACT.Exp).then_inc(GA.sem, 1)
                act.wait_ge(GV.sem, GV.after("arg", i))
                nc.scalar.activation(kd_last[:], kd_last[:], ACT.Exp)
                nc.scalar.activation(at_l, at_l, ACT.Exp).then_inc(GA.sem, 1)
                for l in range(1, LEVELS):
                    act.wait_ge(GP.sem, GP.after(f"y{l}", i))
                    nc.scalar.activation(ym.rearrange("p n t -> p (n t)"), ps[0:CH, BK_1, 0:LP], ACT.Copy
                                         ).then_inc(GA.sem, 1)
                act.wait_ge(GP.sem, GP.after("w", i))
                nc.scalar.activation(wneg, ps[:, BK_1, 0:LP], ACT.Copy, scale=-1.0).then_inc(GA.sem, 1)
                act.wait_ge(GP.sem, GP.after("o2", i))
                nc.scalar.activation(kq[:, 2, 0:T], ps[:, BK_0, 0:T], ACT.Square).then_inc(GA.sem, 1)
                act.wait_ge(GP.sem, GP.after("osum", i))
                nc.scalar.activation(kq[:, 2, 0:T], ps[:, BK_1, 0:T], ACT.Ln, scale=1.0 / P, bias=eps_col[:, 0:1]
                                     ).then_inc(GA.sem, 1)
                act.wait_ge(GA.sem, GA.after("oln", i))
                nc.scalar.activation(kq[:, 2, 0:T], kq[:, 2, 0:T], ACT.Exp, scale=-0.5).then_inc(GA.sem, 1)
                act.wait_ge(GV.sem, GV.after("om1", i))
                apart()
                nc.scalar.activation(y_hi[:, ds1(HEADS + i), :], kq[:, 1, 0:T], ACT.Copy).then_inc(GA.sem, 1)

            def head(i, last):
                head_tiles(i, last)
                attend(i)
                delta(i)

            with act.Fori(0, HEADS) as i:
                head(i, False)

            out_proj("mix_out", 1, FULL, FULL, 1)

            def ffn(layer, norm):
                w = T - FROM[norm]
                for half in range(2):
                    n = 2 * layer + half
                    if half == 0:
                        fill_x(norm, False)

                    def mid_hi_of(j, slot):
                        act.wait_ge(mid_ready, HALF * n + j + 1)
                        apart()
                        nc.scalar.activation(mid_hi[:, bass.ds(j * w, w)], ffn_m[:, slot, 0:w], ACT.Copy
                                             ).then_inc(mid_hi_ready, 1)

                    def body(i, last):
                        for s in range(2):
                            j = 2 * i + s
                            split_next(f"up{n}", i, 2 * s, 4, FULL)
                            act.wait_ge(drained, st[f"up{n}"][2] + 4 * i + 2 * s + 1)
                            nc.scalar.activation(ffn_g[:, s, 0:w], ffn_g[:, s, 0:w], ACT.Silu).then_inc(gate_silu, 1)
                            split_next(f"up{n}", i, 2 * s + 1, 4, FFN_W if last and s else FULL)
                            mid_hi_of(j, s)
                    rounds(act, HALF // 2, body)
                    more = layer == 0 or half == 0
                    out_proj(f"down{n}", 2, FFN_W, FULL if more else None, norm + 1 if half else None)

            ffn(0, 2)

            fill_x(4, False)
            base, _, tile0 = st["ret_in"]
            act.wait_ge(const1_in, CONSTS1)
            act.wait_ge(rel_in, 16)

            def ret_round(i, last):
                def copy_v(j):
                    act.wait_ge(RP.sem, RP.after(f"vt{j}", i))
                    nc.scalar.activation(v_rows[:, 0:2, j * P:(j + 1) * P],
                                         ps[:, BK_D1, 0:2 * P].rearrange("p (b t) -> p b t", b=2), ACT.Copy)
                    nc.scalar.activation(v_rows[0:16, 2, j * P:(j + 1) * P], ps[0:16, BK_D1, 2 * P:3 * P], ACT.Copy
                                         ).then_inc(RA.sem, 1)

                def silu_g(j):
                    act.wait_ge(drained, tile0 + 12 * i + 8 + j + 1)
                    nc.scalar.activation(ret_g[:, j], ret_g[:, j], ACT.Silu).then_inc(RA.sem, 1)

                for s in range(12):
                    split_next("ret_in", i, s, 12, FULL)
                    if s == 3:
                        if not (isinstance(i, int) and i == 0):
                            act.wait_ge(RV.sem, RV.after("s2", i - 1))
                            apart()
                        nc.scalar.activation(dmask, rel, ACT.Exp, scale=lg[:, ds1(i)]).then_inc(RA.sem, 1)
                    if s in (6, 7):
                        copy_v(s - 6)
                    if s == 8:
                        copy_v(2)
                    if s == 9:
                        copy_v(3)
                        silu_g(0)
                    if s == 10:
                        silu_g(1)
                        act.wait_ge(RP.sem, RP.after("o", i))
                        nc.scalar.activation(ret_sq[:].rearrange("p j t -> p (j t)"),
                                             ps[:, BK_0:BK_1 + 1].rearrange("p b t -> p (b t)"), ACT.Square
                                             ).then_inc(RA.sem, 1)
                    if s == 11:
                        silu_g(2)
                        act.wait_ge(RP.sem, RP.after("osum", i))
                        nc.scalar.activation(ret_r[:], ps[:, BK_2, 0:SEQ], ACT.Sqrt, scale=1.0 / (4 * P),
                                             bias=eps_col[:, 0:1]).then_inc(RA.sem, 1)
                        silu_g(3)
                        act.wait_ge(RV.sem, RV.after("y", i))
                        apart()
                        nc.scalar.activation(mid_hi[:, bass.ds(i * 4 * SEQ, 4 * SEQ)],
                                             ret_sq[:].rearrange("p j t -> p (j t)"), ACT.Copy).then_inc(RA.sem, 1)

            ret_round(0, False)
            with act.Fori(1, HEADS) as i:
                ret_round(i, False)
            out_proj("ret_out", 2, FULL, FULL, 5)
            ffn(1, 6)

        @block.vector
        def _(dve):
            V = nc.vector

            def split_lo(slot, width, piece):
                dve.wait_ge(hi_ready, piece + 1)
                V.tensor_tensor(w_lo[:, slot, 0:width], raw[:, slot, 0:width], w_hi[:, slot, 0:width],
                                ALU.subtract).then_inc(lo_ready, 1)

            def split_next(stage, i, q, per_round, width):
                split_lo((q + 1) % 2, width, st[stage][0] + per_round * i + q + 1)

            def take_r(norm, dst):
                t0 = FROM[norm]
                dve.wait_ge(rooted, norm + 1)
                V.reciprocal(dst[:, t0:T], root[:, t0:T]).then_inc(r_ready, 1)
                dve.wait_ge(r_ready, norm + 1)

            def fill_x(norm):
                t0 = FROM[norm]

                def chunk(k):
                    dve.wait_ge(x_hi_ready, KC * (norm // 2) + k + 1)
                    V.scalar_tensor_tensor(x_lo[:, ds1(k), t0:T], h[:, ds1(k), t0:T], gains[:, norm, ds1(k)],
                                           x_hi[:, ds1(k), t0:T], ALU.mult, ALU.subtract).then_inc(x_lo_ready, 1)
                with dve.Fori(0, KC) as k:
                    chunk(k)
                take_r(norm, r_pre)

            def out_proj(stage, n_sub, width, next_width, t0, add, norm):
                _, sig, _ = st[stage]

                def body(i, last):
                    for s in range(2):
                        for sub in range(n_sub):
                            q = n_sub * s + sub
                            w = next_width if last and q == 2 * n_sub - 1 else width
                            if w:
                                split_next(stage, i, q, 2 * n_sub, w)
                        dve.wait_ge(products, sig + 2 * n_sub * i + n_sub * (s + 1))
                        dst = u[:, ds1(2 * i + s), t0:T]
                        if add:
                            V.tensor_tensor(dst, dst, ps[:, s, t0:T], ALU.add).then_inc(drained, 1)
                        else:
                            V.tensor_copy(dst, ps[:, s, t0:T]).then_inc(drained, 1)
                rounds(dve, 8, body)
                if norm is not None:
                    take_r(norm, r_post)
                    with dve.Fori(0, KC) as k:
                        V.scalar_tensor_tensor(u[:, ds1(k), t0:T], u[:, ds1(k), t0:T], gains[:, norm, ds1(k)],
                                               r_post[:, t0:T], ALU.mult, ALU.mult).then_inc(scaled, 1)

            dve.wait_ge(const_in, CONSTS0)
            dve.wait_ge(cleared, 1)
            split_lo(0, FULL, 0)
            fill_x(0)
            for q in range(8):
                split_lo((q + 1) % 2, FULL, q + 1)
                dve.wait_ge(products, q + 1)
                V.tensor_tensor(lat[:, q], ps[:, q % 2, 0:T], r_pre[:], ALU.mult).then_inc(drained, 1)

            dve.wait_ge(LA.sem, LA.after("rooted"))
            V.reciprocal(conv_acc[:], conv_acc[:]).then_inc(LV.sem, 1)
            dve.wait_ge(LV.sem, LV.after("recip"))
            for k in range(4):
                last = V.scalar_tensor_tensor(lat[:, k], lat[:, k], lat_gain[:, k:k + 1], conv_acc[:, 0],
                                              ALU.mult, ALU.mult)
            last.then_inc(LV.sem, 1)
            V.scalar_tensor_tensor(kidx[:], lat[:, 6], lat_gain[:, 6:7], conv_acc[:, 2], ALU.mult, ALU.mult)
            for k in range(4, 6):
                last = V.scalar_tensor_tensor(lat[:, k], lat[:, k], lat_gain[:, k:k + 1], conv_acc[:, 1],
                                              ALU.mult, ALU.mult)
            last.then_inc(LV.sem, 1)
            dve.wait_ge(LA.sem, LA.after("hi_kv"))
            V.tensor_tensor(cq_lo[:], lat[:, 0:4], cq_hi[:], ALU.subtract)
            V.tensor_tensor(ckv_lo[:, :, 0:T], lat[:, 4:6], ckv_hi[:, :, 0:T], ALU.subtract).then_inc(LV.sem, 1)
            V.tensor_copy(gsel[:, 0, 0:T], lat[64:64 + HEADS, 7])
            V.tensor_copy(gb8[:, 1, 0:T], lat[32:32 + HEADS, 7]).then_inc(LV.sem, 1)
            dve.wait_ge(LV.sem, LV.after("shifted"))
            V.tensor_scalar(gsel[:, 0, 0:T], gsel[:, 0, 0:T], decay8[:, 1:2], None, ALU.add).then_inc(LV.sem, 1)
            dve.wait_ge(LV.sem, LV.after("dt"))
            V.tensor_scalar(gb8[:, 0, 0:T], gsel[:, 0, 0:T], 0.0, None, ALU.max).then_inc(LV.sem, 1)
            V.scalar_tensor_tensor(gsel[:, 1, 0:T], gsel[:, 0, 0:T], -1.0, gsel[:, 0, 0:T], ALU.mult, ALU.min
                                   ).then_inc(LV.sem, 1)
            dve.wait_ge(LA.sem, LA.after("beta_exp"))
            V.tensor_scalar(gb8[:, 1, 0:T], gb8[:, 1, 0:T], 1.0, None, ALU.add).then_inc(LV.sem, 1)
            dve.wait_ge(LV.sem, LV.after("one"))
            V.reciprocal(gb8[:, 1, 0:T], gb8[:, 1, 0:T]).then_inc(LV.sem, 1)
            dve.wait_ge(LA.sem, LA.after("ln"))
            V.tensor_tensor(gb8[:, 0, 0:T], gb8[:, 0, 0:T], gsel[:, 1, 0:T], ALU.add).then_inc(LV.sem, 1)
            dve.wait_ge(LA.sem, LA.after("a_exp"))
            V.tensor_scalar(decay8[:, 3:4], decay8[:, 2:3], -1.0, None, ALU.mult).then_inc(LV.sem, 1)
            dve.wait_ge(LV.sem, LV.after("nea"))
            V.tensor_scalar(gsel[:, 0, 0:T], gb8[:, 0, 0:T], decay8[:, 3:4], None, ALU.mult).then_inc(LV.sem, 1)
            dve.wait_ge(LV.sem, LV.after("decay"))
            for n in range(NCH):
                c = slice(n * CH, (n + 1) * CH)
                V.tensor_tensor_scan(gb8[:, 0, c], ones[0:HEADS, 0:CH], gsel[:, 0, c], 0.0, ALU.mult, ALU.add
                                     ).then_inc(LV.sem, 1)
            dve.wait_ge(LP_.sem, LP_.after("index_w"))
            w_scale = (IDX_HEADS * IDX_DIM) ** -0.5
            V.tensor_scalar(widx[:, 0:2], ps[:, BK_1, 0:32].rearrange("p (b t) -> p b t", b=2), w_scale, None,
                            ALU.mult)
            V.tensor_scalar(widx[0:16, 2], ps[0:16, BK_1, 32:48], w_scale, None, ALU.mult).then_inc(LV.sem, 1)
            dve.wait_ge(LP_.sem, LP_.after("columns"))
            V.tensor_copy(cols[:, 0:2].rearrange("p a n t -> p (a n t)"), ps[0:CH, BK_2, 0:2 * NCH * HEADS]
                          ).then_inc(LV.sem, 1)
            dve.wait_ge(LA.sem, LA.after("decayed"))
            V.tensor_tensor(cols[:, 3], cols[:, 1], cols[:, 2], ALU.mult).then_inc(LV.sem, 1)

            base, sig, _ = st["index_q"]
            for t in range(8):
                if t % 4 == 0:
                    split_lo((t // 4 + 1) % 2, FULL, base + t // 4 + 1)
                dve.wait_ge(products, sig + t + 1)
                V.tensor_copy(q_index[:, t], ps[:, t % 2, 0:T]).then_inc(drained, 1)
            for b, (q0, n) in enumerate(BLK):
                c0, keys = ROW[b]
                acc = bias[0:n, c0:c0 + keys]
                for i in range(IDX_HEADS):
                    c = IDX_HEADS * b + i
                    dve.wait_ge(relued, c + 1)
                    part, w = conv_acc[0:n, c % 2, 0:keys], widx[0:n, b, i:i + 1]
                    if i == 0:
                        V.tensor_scalar(acc, part, w, None, ALU.mult).then_inc(scored, 1)
                    else:
                        dve.wait_ge(scored, c)
                        V.scalar_tensor_tensor(acc, part, w, acc, ALU.mult, ALU.add).then_inc(scored, 1)
                dve.wait_ge(TG.sem, TG.after("causal", b))
                for m in range(TOPK // 8):
                    V.max(top8[0:n, :], acc).then_inc(TV.sem, 1)
                    dve.wait_ge(TV.sem, TV.after(f"m{m}", b))
                    V.match_replace(acc, top8[0:n, :], acc, TAKEN).then_inc(TV.sem, 1)
                    dve.wait_ge(TV.sem, TV.after(f"r{m}", b))
                V.tensor_scalar(acc, acc, TAKEN_EDGE, MASKED, ALU.is_gt, ALU.mult).then_inc(TV.sem, 1)
            dve.wait_ge(TG.sem, TG.after("final", 2))

            base, sig, tile0 = st["heads"]

            def head_tiles(i):
                for s in range(6):
                    split_lo((s + 1) % 2, FULL if s in (5, 0, 1, 2) else 4 * P, base + 6 * i + s + 1)
                    dve.wait_ge(products, sig + 7 * i + s + 1)
                    tile = ps[:, s % 2, 0:T]
                    if s < 3:
                        V.tensor_tensor(conv_in[:, s, 3:3 + T], tile, r_pre[:], ALU.mult).then_inc(drained, 1)
                        dve.wait_ge(drained, tile0 + 6 * i + s + 1)
                        V.tensor_scalar(conv_acc[:, s], conv_in[:, s, 0:T], conv_w[:, ds1(i), s, 0:1], None,
                                        ALU.mult).then_inc(CV.sem, 1)
                        for k in range(1, 4):
                            dve.wait_ge(CV.sem, CV.after(f"t{s}{k - 1}", i))
                            V.scalar_tensor_tensor(conv_acc[:, s], conv_in[:, s, k:k + T], conv_w[:, ds1(i), s, k:k + 1],
                                                   conv_acc[:, s], ALU.mult, ALU.add).then_inc(CV.sem, 1)
                    elif s == 3:
                        V.tensor_tensor(gate[:], tile, r_pre[:], ALU.mult).then_inc(drained, 1)
                    elif s == 4:
                        V.tensor_copy(q_h, tile).then_inc(drained, 1)
                    else:
                        V.tensor_copy(k_h, tile).then_inc(drained, 1)
                        dve.wait_ge(products, sig + 7 * i + 7)
                        V.tensor_copy(v_h[:].rearrange("p b t -> p (b t)"), ps[:, BK_D0, 0:3 * P]).then_inc(DV.sem, 1)

            def attend(i):
                dve.wait_ge(DP.sem, DP.after("logits", i))
                for b, (q0, n) in enumerate(BLK):
                    c0, keys = ROW[b]
                    src = ps[0:n, BK_D0, 128 * b:128 * b + keys] if b < 2 else ps[0:n, BK_D1, 0:keys]
                    last = V.scalar_tensor_tensor(dsa_s[0:n, c0:c0 + keys], src, P ** -0.5, bias[0:n, c0:c0 + keys],
                                                  ALU.mult, ALU.add)
                last.then_inc(DV.sem, 1)
                dve.wait_ge(DV.sem, DV.after("scored", i))
                for b, (q0, n) in enumerate(BLK):
                    c0, keys = ROW[b]
                    last = V.tensor_reduce(mx[0:n, b:b + 1], dsa_s[0:n, c0:c0 + keys], AX.X, ALU.max, negate=True)
                last.then_inc(DV.sem, 1)
                dve.wait_ge(DA.sem, DA.after("exped", i))
                V.reciprocal(rinv[:, 0:2], rs[:, 0:2])
                V.reciprocal(rinv[0:16, 2:3], rs[0:16, 2:3]).then_inc(DV.sem, 1)
                dve.wait_ge(DV.sem, DV.after("recips", i))
                for b, (q0, n) in enumerate(BLK):
                    c0, keys = ROW[b]
                    last = V.tensor_scalar(dsa_s[0:n, c0:c0 + keys], dsa_s[0:n, c0:c0 + keys], rinv[0:n, b:b + 1],
                                           None, ALU.mult)
                last.then_inc(DV.sem, 1)
                dve.wait_ge(DA.sem, DA.after("y_hi", i))
                V.tensor_tensor(y_lo[:, ds1(i), :], ps[:, BK_D1, 0:T], y_hi[:, ds1(i), :], ALU.subtract
                                ).then_inc(DV.sem, 1)

            def delta(i):
                def over(ap2, width):
                    return ap2.to_broadcast([CH, NCH, width])

                def each(ap2):
                    return ap2.unsqueeze(1).to_broadcast([CH, NCH, CH])

                def bank(b):
                    return ps[0:CH, b, 0:LP].rearrange("p (n t) -> p n t", n=NCH)

                def rows(b):
                    return ps[0:CH, b, 0:NCH * P].rearrange("p (n t) -> p n t", n=NCH)

                V.tensor_scalar(gsel[:], gb8[:], ident[0:HEADS, ds1(i)], None, ALU.mult).then_inc(GV.sem, 1)
                dve.wait_ge(GA.sem, GA.after("rnorm", i))
                V.tensor_tensor(kq[:, 0, 0:T], qkv[:, 1, 0:T], kq[:, 3, 0:T], ALU.mult)
                V.scalar_tensor_tensor(kq[:, 1, 0:T], qkv[:, 0, 0:T], P ** -0.5, kq[:, 2, 0:T], ALU.mult, ALU.mult
                                       ).then_inc(GV.sem, 1)
                dve.wait_ge(GV.sem, GV.after("kq", i))
                dve.wait_ge(GA.sem, GA.after("decayed", i))
                V.tensor_tensor(kq[:, 2], kq[:, 0], ps[:, BK_3, 0:LP], ALU.mult)
                V.tensor_tensor(kq[:, 3], kq[:, 1], dec[:], ALU.mult).then_inc(GV.sem, 1)
                for n in range(NCH):
                    V.tensor_scalar(at_l[:, n], ps[0:CH, BK_2, n * CH:(n + 1) * CH], cols[:, 0, n, ds1(i)], 0.0,
                                    ALU.subtract, ALU.min)
                V.tensor_tensor(kd_last[:].unsqueeze(2), bank(BK_2)[:, :, CH - 1:CH], cols[:, 0, :, ds1(i)],
                                ALU.subtract).then_inc(GV.sem, 1)
                dve.wait_ge(GA.sem, GA.after("decmat", i))
                V.tensor_tensor(at_l, at_l, each(upto[:]), ALU.mult).then_inc(GV.sem, 1)
                dve.wait_ge(GP.sem, GP.after("scores", i))
                dve.wait_ge(GV.sem, GV.after("masked", i))
                V.tensor_tensor(at, bank(BK_0), at_l, ALU.mult)
                V.tensor_tensor(qk, bank(BK_1), at_l, ALU.mult).then_inc(GV.sem, 1)
                dve.wait_ge(GP.sem, GP.after("turned", i))
                V.tensor_tensor(kbg, rows(BK_2), over(cols[:, 3, :, ds1(i)], P), ALU.mult)
                V.tensor_tensor(kd, rows(BK_2), over(kd_last[:].unsqueeze(2), P), ALU.mult)
                V.tensor_tensor(vb, rows(BK_3), over(cols[:, 1, :, ds1(i)], P), ALU.mult).then_inc(GV.sem, 1)
                dve.wait_ge(GV.sem, GV.after("mats", i))
                V.tensor_tensor(at_l, at, each(levels[:, 0]), ALU.mult).then_inc(GV.sem, 1)
                dve.wait_ge(GV.sem, GV.after("at0", i))
                V.tensor_tensor(tt, each(ident[0:CH, 0:CH]), at_l, ALU.subtract).then_inc(GV.sem, 1)
                dve.wait_ge(GP.sem, GP.after("tm0", i))
                V.tensor_copy(tm, bank(BK_0)).then_inc(GV.sem, 1)
                for l in range(1, LEVELS):
                    dve.wait_ge(GP.sem, GP.after(f"z{l}", i))
                    if l < LEVELS - 1:
                        V.tensor_tensor(tm, tm, bank(BK_0), ALU.subtract).then_inc(GV.sem, 1)
                    V.tensor_tensor(tt, tt, bank(BK_2), ALU.subtract).then_inc(GV.sem, 1)
                for n in range(NCH):
                    dve.wait_ge(GP.sem, GP.after(f"v{n}", i))
                    V.tensor_copy(v_new[:, n], ps[0:CH, BK_3, n * P:(n + 1) * P]).then_inc(GV.sem, 1)
                    if n < NCH - 1:
                        dve.wait_ge(GP.sem, GP.after(f"o{n}", i))
                        if n == 0:
                            V.tensor_copy(state[:], ps[:, BK_2, 0:P]).then_inc(GV.sem, 1)
                        else:
                            V.scalar_tensor_tensor(state[:], state[:], dec[:, (n + 1) * CH - 1:(n + 1) * CH],
                                                   ps[:, BK_2, 0:P], ALU.mult, ALU.add).then_inc(GV.sem, 1)
                dve.wait_ge(GA.sem, GA.after("ornorm", i))
                V.scalar_tensor_tensor(kq[:, 1, 0:T], ps[:, BK_0, 0:T], lat_gain[:, 7:8], kq[:, 2, 0:T],
                                       ALU.mult, ALU.mult).then_inc(GV.sem, 1)
                dve.wait_ge(CA.sem, CA.after("gate", i))
                dve.wait_ge(GV.sem, GV.after("om0", i))
                V.tensor_tensor(kq[:, 1, 0:T], kq[:, 1, 0:T], gate[:], ALU.mult).then_inc(GV.sem, 1)
                dve.wait_ge(GA.sem, GA.after("y_hi", i))
                V.tensor_tensor(y_lo[:, ds1(HEADS + i), :], kq[:, 1, 0:T], y_hi[:, ds1(HEADS + i), :], ALU.subtract
                                ).then_inc(GV.sem, 1)

            with dve.Fori(0, HEADS) as i:
                head_tiles(i)
                attend(i)
                delta(i)

            out_proj("mix_out", 1, FULL, FULL, 0, False, 1)

            def ffn(layer, norm):
                t0 = FROM[norm]
                w = T - t0
                for half in range(2):
                    n = 2 * layer + half
                    if half == 0:
                        fill_x(norm)
                    _, sig, _ = st[f"up{n}"]

                    def body(i, last):
                        for s in range(2):
                            j = 2 * i + s
                            split_next(f"up{n}", i, 2 * s, 4, FULL)
                            dve.wait_ge(products, sig + 4 * i + 2 * s + 1)
                            V.tensor_tensor(ffn_g[:, s, 0:w], ps[:, 0, t0:T], r_pre[:, t0:T], ALU.mult
                                            ).then_inc(drained, 1)
                            split_next(f"up{n}", i, 2 * s + 1, 4, FFN_W if last and s else FULL)
                            dve.wait_ge(products, sig + 4 * i + 2 * s + 2)
                            V.tensor_tensor(ffn_m[:, s, 0:w], ps[:, 1, t0:T], r_pre[:, t0:T], ALU.mult
                                            ).then_inc(drained, 1)
                            dve.wait_ge(drained, st[f"up{n}"][2] + 4 * i + 2 * s + 2)
                            dve.wait_ge(gate_silu, HALF * n + j + 1)
                            V.tensor_tensor(ffn_m[:, s, 0:w], ffn_m[:, s, 0:w], ffn_g[:, s, 0:w], ALU.mult
                                            ).then_inc(mid_ready, 1)
                            dve.wait_ge(mid_hi_ready, HALF * n + j + 1)
                            V.tensor_tensor(mid_lo[:, bass.ds(j * w, w)], ffn_m[:, s, 0:w],
                                            mid_hi[:, bass.ds(j * w, w)], ALU.subtract).then_inc(mid_lo_ready, 1)
                    rounds(dve, HALF // 2, body)
                    more = layer == 0 or half == 0
                    out_proj(f"down{n}", 2, FFN_W, FULL if more else None, t0, half == 1,
                             norm + 1 if half else None)

            ffn(0, 2)

            fill_x(4)
            dve.wait_ge(const1_in, CONSTS1)
            for c in range(2):
                last = V.tensor_tensor(rope[:, c], rope[:, c], r_pre[:], ALU.mult)
            last.then_inc(rope_ready, 1)
            dve.wait_ge(rope_ready, 1)
            base, sig, tile0 = st["ret_in"]

            def ret_round(i):
                first = isinstance(i, int) and i == 0
                for s in range(12):
                    split_next("ret_in", i, s, 12, FULL)
                    if s == 11:
                        dve.wait_ge(RA.sem, RA.after("rooted", i))
                        V.reciprocal(ret_r[:], ret_r[:]).then_inc(RV.sem, 1)
                    dve.wait_ge(products, sig + 12 * i + s + 1)
                    t0 = META if s < 2 else 0
                    tile = ps[:, s % 2, t0:T]
                    if s in (0, 2):
                        if s == 2:
                            dve.wait_ge(RG.sem, RG.after("q", i))
                        elif not first:
                            dve.wait_ge(RG.sem, RG.after("k", i - 1))
                        V.tensor_tensor(rot_a[:, 0, t0:T], tile, rope[:, 0, t0:T], ALU.mult)
                        V.tensor_tensor(rot_a[:, 1, t0:T], tile, rope[:, 1, t0:T], ALU.mult).then_inc(drained, 1)
                    elif s in (1, 3):
                        dst = q_rot if s == 1 else k_rot
                        V.tensor_tensor(dst[:, 0], tile, rope[:, 1, t0:T], ALU.mult)
                        V.tensor_tensor(dst[:, 1], tile, rope[:, 0, t0:T], ALU.mult).then_inc(drained, 1)
                    elif s < 8:
                        if s > 4:
                            dve.wait_ge(RP.sem, RP.after(f"vt{s - 5}", i))
                        V.tensor_tensor(v_t, tile, r_pre[:], ALU.mult).then_inc(drained, 1)
                    else:
                        V.tensor_tensor(ret_g[:, s - 8], ps[:, s % 2, META:T], r_pre[:, META:T], ALU.mult
                                        ).then_inc(drained, 1)
                    if s == 8:
                        dve.wait_ge(RP.sem, RP.after("scores", i))
                        dve.wait_ge(RA.sem, RA.after("dmask", i))
                        V.scalar_tensor_tensor(ret_s[:, 0:400], ps[:, BK_D0, 0:400], (2 * P) ** -0.5, dmask[:, 0:400],
                                               ALU.mult, ALU.mult).then_inc(RV.sem, 1)
                        V.scalar_tensor_tensor(ret_s[0:16, 400:416], ps[0:16, BK_D0, 400:416], (2 * P) ** -0.5,
                                               dmask[0:16, 400:416], ALU.mult, ALU.mult).then_inc(RV.sem, 1)
                dve.wait_ge(RV.sem, RV.after("recip", i))
                dve.wait_ge(RA.sem, RA.after("g3", i))
                V.tensor_tensor(ret_g, ret_g, ret_r[:].unsqueeze(1).to_broadcast([P, 4, SEQ]), ALU.mult
                                ).then_inc(RV.sem, 1)
                dve.wait_ge(RV.sem, RV.after("gr", i))
                dve.wait_ge(RP.sem, RP.after("osum", i))
                V.tensor_tensor(ret_sq[:].rearrange("p j t -> p (j t)"),
                                ps[:, BK_0:BK_1 + 1].rearrange("p b t -> p (b t)"),
                                ret_g.rearrange("p j t -> p (j t)"), ALU.mult).then_inc(RV.sem, 1)
                dve.wait_ge(RA.sem, RA.after("y_hi", i))
                V.tensor_tensor(mid_lo[:, bass.ds(i * 4 * SEQ, 4 * SEQ)], ret_sq[:].rearrange("p j t -> p (j t)"),
                                mid_hi[:, bass.ds(i * 4 * SEQ, 4 * SEQ)], ALU.subtract).then_inc(RV.sem, 1)

            ret_round(0)
            with dve.Fori(1, HEADS) as i:
                ret_round(i)
            out_proj("ret_out", 2, FULL, FULL, META, False, 5)
            ffn(1, 6)

        @block.gpsimd
        def _(pool):
            G = nc.gpsimd
            G.memset(eps_col[:, 0:1], EPS)
            G.memset(eps_col[:, 1:2], 1.0)
            G.memset(ckv_hi[:, :, T:3 * P].bitcast(F32), 0.0)
            G.memset(ckv_lo[:, :, T:3 * P].bitcast(F32), 0.0)
            G.memset(conv_in[:, :, 0:3], 0.0)
            G.memset(qkv[:, :, T:LP], 0.0)
            G.memset(kq[:, 0:2, T:LP], 0.0)
            G.memset(gb8[:, :, T:LP], 0.0)
            G.memset(gsel[:, :, T:LP], 0.0).then_inc(cleared, 1)

            for b, (q0, n) in enumerate(BLK):
                c0, keys = ROW[b]
                acc = bias[0:n, c0:c0 + keys]
                pool.wait_ge(scored, IDX_HEADS * (b + 1))
                G.affine_select(out=acc, in_=acc, pattern=[[-1, keys]], compare_op=ALU.is_ge, fill=NONCAUSAL,
                                base=q0, channel_multiplier=1).then_inc(TG.sem, 1)
                pool.wait_ge(TV.sem, TV.after("chosen", b))
                G.affine_select(out=acc, in_=acc, pattern=[[-1, keys]], compare_op=ALU.is_ge, fill=MASKED,
                                base=q0, channel_multiplier=1).then_inc(TG.sem, 1)

            with pool.Fori(0, HEADS) as i:
                for l in range(1, LEVELS):
                    if l == 1:
                        pool.wait_ge(GV.sem, GV.after("tt0", i))
                    else:
                        pool.wait_ge(GP.sem, GP.after(f"y{l - 1}", i))
                    G.tensor_tensor(at_l, at, levels[:, l].unsqueeze(1).to_broadcast([CH, NCH, CH]), ALU.mult
                                    ).then_inc(GG.sem, 1)

            def residual(norm):
                t0 = FROM[norm]
                with pool.Fori(0, KC) as k:
                    pool.wait_ge(scaled, KC * (norm // 2) + k + 1)
                    G.tensor_tensor(h[:, ds1(k), t0:T], h[:, ds1(k), t0:T], u[:, ds1(k), t0:T], ALU.add
                                    ).then_inc(h_ready, 1)

            residual(1)
            residual(3)
            pool.wait_ge(h_ready, 2 * KC)
            pool.dma_start(rel, a["rel"]).then_inc(rel_in, 16)
            _, _, tile0 = st["ret_in"]
            with pool.Fori(0, HEADS) as i:
                for s, (dst, t0) in enumerate(((q_rot, META), (k_rot, 0))):
                    pool.wait_ge(drained, tile0 + 12 * i + 2 * s + 2)
                    G.tensor_tensor(dst[:, 0], rot_a[:, 0, t0:T], dst[:, 0], ALU.subtract)
                    G.tensor_tensor(dst[:, 1], rot_a[:, 1, t0:T], dst[:, 1], ALU.add).then_inc(RG.sem, 1)
            residual(5)
            residual(7)


def tiles16(w):
    k, m = w.shape
    return w.reshape(k // P, P, m // P, P).transpose(2, 1, 0, 3).reshape(m // P, P, k // P * P)


def by_chunk(v):
    return v.reshape(-1, P).T


def kernel(**inputs):
    import concourse.bacc as bacc
    from concourse.bass_utils import run_bass_kernel_spmd

    g = {k: np.asarray(v) for k, v in inputs.items()}
    w_in = g["hy_w_in"][0]
    cut = np.cumsum([512, 256, IDX_DIM, IDX_HEADS, 3 * 1024, 1024, HEADS, HEADS])
    c_q, c_kv, k_idx, w_idx, qkv, z, beta, a_raw = np.split(w_in, cut[:-1], axis=1)
    zero = np.zeros((D, P), np.float32)
    rest = zero.copy()
    rest[:, 0:16], rest[:, 32:40], rest[:, 64:72] = w_idx, beta, a_raw
    arrays = {
        "x_t": np.concatenate([g["meta_tokens"], g["x"][0]], 0).T.reshape(KC, P, T).transpose(1, 0, 2),
        "w_latent": tiles16(np.concatenate([c_q, c_kv, k_idx, k_idx, rest], 1)),
    }
    arrays["w_index_q"] = tiles16(g["dsa_w_qidx"][0]).reshape(2, 4, P, 4 * P).transpose(0, 2, 1, 3).reshape(2, P, 16 * P)
    parts = [tiles16(m) for m in (qkv[:, :1024], qkv[:, 1024:2048], qkv[:, 2048:], z)]
    arrays["w_heads"] = np.stack(parts, 1).reshape(4 * HEADS, P, 16 * P)
    kv = tiles16(g["dsa_w_ukv"][0]).reshape(HEADS, 2, P, 2 * P).transpose(0, 2, 1, 3).reshape(HEADS, P, 4 * P)
    arrays["w_dsa"] = np.stack([tiles16(g["dsa_w_uq"][0]), kv], 1).reshape(2 * HEADS, P, 4 * P)
    arrays["w_mix_out"] = tiles16(g["hy_w_out"][0])
    up, down = [], []
    for layer in range(2):
        gate_up = np.stack([tiles16(g["ffn_w_gate"][layer]), tiles16(g["ffn_w_up"][layer])], 1)
        up.append(gate_up.reshape(4 * HALF, P, 16 * P))
        wd = tiles16(g["ffn_w_down"][layer]).reshape(KC, P, 2, 2, SUB * P).transpose(2, 0, 3, 1, 4)
        down.append(wd.reshape(4 * KC, P, SUB * P))
    arrays["w_up"], arrays["w_down"] = np.concatenate(up), np.concatenate(down)
    q, k, v, gt = np.split(g["ret_w_in"][0], [D, 2 * D, 2 * D + 4096], axis=1)

    def pairs(m):
        return m.reshape(D, HEADS, P, 2).transpose(0, 1, 3, 2).reshape(D, HEADS, 2 * P)

    ret = np.concatenate([pairs(q), pairs(k), v.reshape(D, HEADS, 512), gt.reshape(D, HEADS, 512)], 2)
    arrays["w_ret_in"] = tiles16(ret.reshape(D, HEADS * 12 * P))
    arrays["w_ret_out"] = tiles16(g["ret_w_out"][0]).reshape(KC, P, 2, KC * P).transpose(0, 2, 1, 3).reshape(2 * KC, P, KC * P)
    norms = [g[n][l] for l in range(2) for n in ("mix_norm_pre", "mix_norm_post", "ffn_norm_pre", "ffn_norm_post")]
    arrays["gains"] = np.stack([by_chunk(n) for n in norms], 1)
    kn = g["dsa_kidx_norm"][0]
    arrays["lat_gain"] = np.concatenate([by_chunk(g["dsa_q_norm"][0]), by_chunk(g["dsa_kv_norm"][0]),
                                         np.concatenate([kn, kn])[:, None], g["gdn_o_norm"][0][:, None]], 1)
    cw = g["gdn_conv_w"][0].reshape(4, 3, HEADS, P)
    arrays["conv_w"] = cw.transpose(3, 2, 1, 0)
    arrays["decay8"] = np.stack([g["gdn_a_log"][0], g["gdn_dt_bias"][0]], 1)
    arrays["ones"] = np.ones((P, P), np.float32)
    arrays["ident"] = np.eye(P, dtype=np.float32)
    j, i = np.arange(CH)[:, None], np.arange(CH)[None, :]
    arrays["levels"] = np.stack([((i >> l) % 2 == 1) & ((j >> l) == (i >> l) - 1) for l in range(LEVELS)], 1).astype(np.float32)
    arrays["upto"] = (j <= i).astype(np.float32)
    inv = 1.0 / (np.float32(10000.0) ** np.linspace(0.0, 1.0, P, dtype=np.float32))
    ang = np.arange(T, dtype=np.float32)[None, :] * inv.astype(np.float32)[:, None]
    arrays["rope"] = np.stack([np.cos(ang), np.sin(ang)], 1).astype(np.float32)
    log_gamma = np.log(1.0 - 2.0 ** (-5.0 - np.arange(HEADS)))
    arrays["log_gamma"] = np.tile(log_gamma.astype(np.float32), (P, 1))
    rel = np.full((P, 416), 1.0e9, np.float32)
    for (c0, q0, nq), (k0, nk) in zip(RROW, BLK):
        dist = (META + q0 + np.arange(nq))[None, :] - (k0 + np.arange(nk))[:, None]
        rel[:nk, c0:c0 + nq] = np.where(dist >= 0, dist, 1.0e9)
    arrays["rel"] = rel
    arrays = {k: np.ascontiguousarray(v) for k, v in arrays.items()}

    nc = bacc.Bacc("TRN2", target_bir_lowering=False, num_devices=1)
    aps = {k: nc.dram_tensor(f"in_{k}", v.shape, mybir.dt.from_np(v.dtype), kind="ExternalInput").ap()
           for k, v in arrays.items()}
    out = nc.dram_tensor("out_t", (P, KC, SEQ), F32, kind="ExternalOutput").ap()
    trunk(nc, aps, out)
    r = run_bass_kernel_spmd(nc, [{f"in_{k}": v for k, v in arrays.items()}], core_ids=[0])
    res = r.results[0]["out_t"]
    return res.transpose(1, 0, 2).reshape(D, SEQ).T[None]
```

```python
from contextlib import ExitStack

import numpy as np
import concourse.bass as bass
from concourse import mybir

F32 = mybir.dt.float32
F32R = mybir.dt.float32r
ACT = mybir.ActivationFunctionType
ALU = mybir.AluOpType
AX = mybir.AxisListType

P = 128
D = 2048
META = 16
SEQ = 256
T = META + SEQ
KC = D // P
DFF = 5632
HEADS = 8
EPS = 1e-6
BLK = [(0, 128), (128, 128), (256, 16)]
ROW = [(0, 128), (128, 256), (384, 272)]
ROWS_W = 656
TOPK = 64
IDX_HEADS = 16
IDX_DIM = 64
CH = 91
NCH = 3
LP = CH * NCH
LEVELS = 7
HALF = DFF // P // 2
SUB = HALF // 2
TROW = [(0, 0, 272), (272, 128, 144), (416, 256, 16)]
RROW = [(0, 0, 256), (256, 112, 144), (400, 240, 16)]
MASKED = -1.0e30
NONCAUSAL = -3.0e38
TAKEN = -3.4e38
TAKEN_EDGE = -3.3e38


def stage_table():
    table, at = {}, [0, 0, 0]
    for name, *sizes in (
            ("latent", 8, 16, 8), ("mixer", 6 * HEADS + 2, 11 * HEADS + 8, 6 * HEADS + 8),
            ("mix_out", 16, 32, 16),
            ("up0", 2 * HALF, 4 * HALF, 2 * HALF), ("down0", 32, 64, 16),
            ("up1", 2 * HALF, 4 * HALF, 2 * HALF), ("down1", 32, 64, 16),
            ("ret_in", 12 * HEADS, 24 * HEADS, 12 * HEADS), ("ret_out", 32, 64, 16),
            ("up2", 2 * HALF, 4 * HALF, 2 * HALF), ("down2", 32, 64, 16),
            ("up3", 2 * HALF, 4 * HALF, 2 * HALF), ("down3", 32, 64, 16), ("end", 0, 0, 0)):
        table[name] = tuple(at)
        at = [x + y for x, y in zip(at, sizes)]
    return table


LAG = 3
INDEX_Q = (12, 24, 12)


def head_at(i):
    if isinstance(i, int) and i < LAG:
        return [(8, 16, 8, 4), (14, 32, 20, 7), (18, 40, 24, 9)][i]
    return 6 * i + 6, 11 * i + 18, 6 * i + 12, 3 * i + 3


def dsa_at(a):
    if isinstance(a, int) and a > HEADS - LAG:
        d = a - (HEADS - LAG)
        return 52 + 2 * d, 103 + 3 * d, 58 + 2 * d, 26 + d
    return 6 * a + 22, 11 * a + 48, 6 * a + 28, 3 * a + 11


class Steps:

    def __init__(self, sem, names):
        self.sem, self.names = sem, names.split()

    def after(self, name, rnd=0):
        return rnd * len(self.names) + (self.names.index(name) + 1)


def trunk(nc, a, out):
    ctx = ExitStack()
    st = stage_table()
    with ctx:
        def sb(name, shape, dt=F32, c=ctx):
            return c.enter_context(nc.sbuf_tensor(name, shape, dt))

        def sem(name):
            return ctx.enter_context(nc.semaphore(name))

        h = sb("h", [P, KC, T])
        x_hi = sb("x_hi", [P, KC, T], F32R)
        x_lo = sb("x_lo", [P, KC, T], F32R)
        u = sb("u", [P, KC, T])
        raw = sb("raw", [P, 2, 16 * P])
        w_hi = sb("w_hi", [P, 2, 16 * P], F32R)
        w_lo = sb("w_lo", [P, 2, 16 * P], F32R)
        gains = sb("gains", [P, 8, KC])
        ones = sb("ones", [P, P])
        ident = sb("ident", [P, P])
        sq = sb("sq", [P, 2, T])
        r_pre = sb("r_pre", [P, T])
        r_post = sb("r_post", [P, T])
        sq_sum = sb("sq_sum", [P, T])
        eps_col = sb("eps_col", [P, 2])
        scratch = sb("scratch", [P, 2])
        flat = u[:, :, :].rearrange("p c t -> p (c t)")
        with ExitStack() as early:
            q_index = sb("q_index", [P, 8, T], F32, early)
        with ExitStack() as first:
            y_hi = sb("y_hi", [P, KC, T], F32R, first)
            y_lo = sb("y_lo", [P, KC, T], F32R, first)
            cq_hi = sb("cq_hi", [P, 4, T], F32R, first)
            cq_lo = sb("cq_lo", [P, 4, T], F32R, first)
            ckv_hi = sb("ckv_hi", [P, 2, 3 * P], F32R, first)
            ckv_lo = sb("ckv_lo", [P, 2, 3 * P], F32R, first)
            kidx = sb("kidx", [P, T], F32, first)
            bias = sb("bias", [P, ROWS_W], F32, first)
            lat_gain = sb("lat_gain", [P, 8], F32, first)
            widx = sb("widx", [P, 3, IDX_HEADS], F32, first)
            levels = sb("levels", [CH, LEVELS, CH], F32, first)
            upto = sb("upto", [CH, CH], F32, first)
            conv_w = sb("conv_w", [P, HEADS, 3, 4], F32, first)
            gb8 = sb("gb8", [HEADS, 2, LP], F32, first)
            gsel = sb("gsel", [HEADS, 2, LP], F32, first)
            decay8 = sb("decay8", [HEADS, 4], F32, first)
            cols = sb("cols", [CH, 4, NCH, HEADS], F32, first)
            conv_in = sb("conv_in", [P, 3, 3 + T], F32, first)
            conv_acc = sb("conv_acc", [P, 3, T], F32, first)
            qkv = sb("qkv", [P, 3, LP], F32, first)
            gate = sb("gate", [P, T], F32, first)
            kq = sb("kq", [P, 4, LP], F32, first)
            dec = sb("dec", [P, LP], F32, first)
            state = sb("state", [P, P], F32, first)
            v_new = sb("v_new", [CH, NCH, P], F32, first)
            kd_last = sb("kd_last", [CH, NCH], F32, first)
            top8 = sb("top8", [P, 8], F32, first)
            mx = sb("mx", [P, 3], F32, first)
            rs = sb("rs", [P, 3], F32, first)
            rinv = sb("rinv", [P, 3], F32, first)
            v_h = sb("v_h", [P, 3, P], F32, first)
            dsa_s = sb("dsa_s", [P, ROWS_W], F32, first)
            p_t = sb("p_t", [P, 432], F32, first)
        with ExitStack() as second:
            mid_hi = sb("mid_hi", [P, 32 * SEQ], F32R, second)
            mid_lo = sb("mid_lo", [P, 32 * SEQ], F32R, second)
            ffn_g = sb("ffn_g", [P, 2, T], F32, second)
            ffn_m = sb("ffn_m", [P, 2, T], F32, second)
            rope = sb("rope", [P, 2, T], F32, second)
            lg = sb("lg", [P, HEADS], F32, second)
            q_rot = sb("q_rot", [P, 2, SEQ], F32, second)
            k_rot = sb("k_rot", [P, 2, T], F32, second)
            rot_a = sb("rot_a", [P, 2, T], F32, second)
            ret_sq = sb("ret_sq", [P, 4, SEQ], F32, second)
            ret_r = sb("ret_r", [P, SEQ], F32, second)

        def carve(cursor, shape):
            n = int(np.prod(shape[1:]))
            part = flat[0:shape[0], cursor[0]:cursor[0] + n]
            cursor[0] += n
            assert cursor[0] <= KC * T
            return part if len(shape) == 2 else part.rearrange("p (x y) -> p x y", x=shape[1])

        c1 = [0]
        lat = carve(c1, [P, 8, T])
        c2 = [0]
        at = carve(c2, [CH, NCH, CH])
        at_l = carve(c2, [CH, NCH, CH])
        qk = carve(c2, [CH, NCH, CH])
        tm = carve(c2, [CH, NCH, CH])
        tt = carve(c2, [CH, NCH, CH])
        ym = carve(c2, [CH, NCH, CH])
        kbg = carve(c2, [CH, NCH, P])
        kd = carve(c2, [CH, NCH, P])
        vb = carve(c2, [CH, NCH, P])
        wneg = carve(c2, [P, LP])
        c3 = list(c2)
        q_h = carve(c3, [P, T])
        k_h = carve(c3, [P, T])
        o_sq = carve(c3, [P, T])
        o_m = carve(c3, [P, T])
        c4 = [0]
        rel = carve(c4, [P, 416])
        dmask = carve(c4, [P, 416])
        ret_s = carve(c4, [P, 416])
        v_rows = carve(c4, [P, 3, 512])
        v_t = carve(c4, [P, T])
        ret_g = carve(c4, [P, 4, SEQ])

        ps = ctx.enter_context(nc.psum_tensor("ps", [P, 8, 512], F32))
        BK_SUM, BK_D0, BK_D1, BK_0, BK_1, BK_2, BK_3 = 2, 2, 3, 4, 5, 6, 7

        h_in = [sem(f"h_in{i}") for i in range(4)]
        gains_in = sem("gains_in")
        ones_in = sem("ones_in")
        const_in = sem("const_in")
        rel_in = sem("rel_in")
        const1_in = sem("const1_in")
        piece_in = [sem("piece_in0"), sem("piece_in1")]
        hi_ready = sem("hi_ready")
        lo_ready = sem("lo_ready")
        products = sem("products")
        drained = sem("drained")
        scaled = sem("scaled")
        h_ready = sem("h_ready")
        x_hi_ready = sem("x_hi_ready")
        x_lo_ready = sem("x_lo_ready")
        squared = sem("squared")
        summed = sem("summed")
        totalled = sem("totalled")
        rooted = sem("rooted")
        r_ready = sem("r_ready")
        gate_silu = sem("gate_silu")
        mid_ready = sem("mid_ready")
        mid_hi_ready = sem("mid_hi_ready")
        mid_lo_ready = sem("mid_lo_ready")
        out_done = sem("out_done")

        LA = Steps(sem("lat_act"), "squared rooted hi_q hi_kv beta_exp exp ln a_exp decayed")
        LP_ = Steps(sem("lat_pe"), "summed index_w columns")
        LV = Steps(sem("lat_dve"), "recip norm_q norm_kv lo shifted dt max abs one packed softplus nea decay "
                   "scan0 scan1 scan2 widx cols01 cols3")
        dots = sem("dots")
        relued = sem("relued")
        scored = sem("scored")
        TV = Steps(sem("top_dve"), " ".join(f"m{i} r{i}" for i in range(TOPK // 8)) + " chosen")
        causal = sem("causal")
        bias_done = sem("bias_done")

        CV = Steps(sem("conv_dve"), "t00 t01 t02 t03 t10 t11 t12 t13 t20 t21 t22 t23")
        CA = Steps(sem("conv_act"), "silu0 silu1 silu2 gate")

        DP = Steps(sem("dsa_pe"), "logits turned attended")
        DV = Steps(sem("dsa_dve"), "scored maxed recips y_lo")
        DA = Steps(sem("dsa_act"), "values exped probs turned y_hi")

        GP = Steps(sem("gdn_pe"), "sums spread scores turned tm0 "
                   + " ".join(f"y{i} z{i} zt{i}" for i in range(1, LEVELS - 1))
                   + f" y{LEVELS - 1} zt{LEVELS - 1} w v0 k0 v1 k1 v2 o2")
        GA = Steps(sem("gdn_act"), "squared ln rnorm decayed decmat tm0 "
                   + " ".join(f"y{i}" for i in range(1, LEVELS)) + " w vn0 vn1 vn2")
        GV = Steps(sem("gdn_dve"), "select kq kb arg masked mats at0 tt0 rows "
                   + " ".join(f"tm{i} tt{i}" for i in range(1, LEVELS - 1)) + f" tt{LEVELS - 1} s0 s1")
        GG = Steps(sem("gdn_pool"), " ".join(f"lev{i}" for i in range(1, LEVELS)))
        FP = Steps(sem("gate_pe"), "osum")
        FA = Steps(sem("gate_act"), "o ln rnorm y_hi")
        FV = Steps(sem("gate_dve"), "om0 om1 y_lo")

        RP = Steps(sem("ret_pe"), "vt0 vt1 vt2 vt3 scores o osum")
        RV = Steps(sem("ret_dve"), "s s2 recip gr y y_lo")
        RA = Steps(sem("ret_act"), "dmask vr0 vr1 vr2 vr3 g0 g1 osq g2 rooted g3 y_hi")
        RG = Steps(sem("ret_pool"), "q k")
        rope_ready = sem("rope_ready")

        cleared = sem("cleared")
        block = ctx.enter_context(nc.Block())

        def ds1(i):
            return bass.ds(i, 1)

        def rounds(eng, n, body, peeled=0):
            if peeled:
                body(0, False)
            with eng.Fori(peeled, n - 1) as i:
                body(i, False)
            body(n - 1, True)

        FFN_W = SUB * P
        FULL = 16 * P
        HALF_W = 8 * P

        def halves(width):
            if width <= HALF_W:
                return [(slice(0, width), 2)]
            return [(slice(0, HALF_W), 1), (slice(HALF_W, width), 1)]


        @block.sync
        def _(sp):
            sp.dma_start(gains[:], a["gains"]).then_inc(gains_in, 16)
            sp.dma_start(raw[:, 0], a["w_latent"][0]).then_inc(piece_in[0], 16)
            for i in range(4):
                sp.dma_start(h[:, 4 * i:4 * i + 4, :], a["x_t"][:, 4 * i:4 * i + 4, :]).then_inc(h_in[i], 16)
                if i == 0:
                    sp.dma_start(ones[:], a["ones"]).then_inc(ones_in, 16)
                if i == 1:
                    sp.dma_start(raw[:, 1], a["w_latent"][1]).then_inc(piece_in[1], 16)
            sp.dma_start(ident[:], a["ident"]).then_inc(const_in, 16)
            sp.dma_start(lat_gain[:, :], a["lat_gain"]).then_inc(const_in, 16)
            sp.dma_start(levels[:], a["levels"]).then_inc(const_in, 16)
            sp.dma_start(upto[:], a["upto"]).then_inc(const_in, 16)
            sp.dma_start(conv_w[:], a["conv_w"]).then_inc(const_in, 16)
            sp.dma_start(decay8[:, 0:2], a["decay8"]).then_inc(const_in, 16)

            def load(slot, width, src, piece):
                sp.wait_ge(lo_ready, 2 * (piece - 1))
                sp.dma_start(raw[:, slot, 0:width], src).then_inc(piece_in[slot], 16)

            base = st["latent"][0]
            with sp.Fori(1, 4) as i:
                for s in range(2):
                    load(s, FULL, a["w_latent"][ds1(2 * i + s)], base + 2 * i + s)
            def load_head(i):
                for s in range(4):
                    load(s % 2, FULL, a["w_heads"][ds1(4 * i + s)], head_at(i)[0] + s)

            def load_dsa(i):
                for s in range(2):
                    load(s, 4 * P, a["w_dsa"][ds1(2 * i + s)], dsa_at(i)[0] + s)

            load_head(0)
            for s in range(2):
                load(s, FULL, a["w_index_q"][s], INDEX_Q[0] + s)
            load_head(1)
            load_head(2)
            with sp.Fori(0, HEADS - LAG) as i:
                load_dsa(i)
                load_head(i + LAG)
            for i in range(HEADS - LAG, HEADS):
                load_dsa(i)
            base = st["mix_out"][0]
            with sp.Fori(0, 8) as i:
                for s in range(2):
                    load(s, FULL, a["w_mix_out"][ds1(2 * i + s)], base + 2 * i + s)

            def ffn(layer):
                for half in range(2):
                    n = 2 * layer + half
                    base = st[f"up{n}"][0]
                    with sp.Fori(0, HALF) as i:
                        for s in range(2):
                            load(s, FULL, a["w_up"][ds1(2 * HALF * n + 2 * i + s)], base + 2 * i + s)
                    base = st[f"down{n}"][0]
                    with sp.Fori(0, KC) as i:
                        for s in range(2):
                            load(s, FFN_W, a["w_down"][ds1(2 * KC * n + 2 * i + s)], base + 2 * i + s)

            ffn(0)
            sp.wait_ge(products, st["mix_out"][1] + 32)
            sp.dma_start(rope[:], a["rope"]).then_inc(const1_in, 16)
            sp.dma_start(lg[:], a["log_gamma"]).then_inc(const1_in, 16)
            base = st["ret_in"][0]
            with sp.Fori(0, 6 * HEADS) as i:
                for s in range(2):
                    load(s, FULL, a["w_ret_in"][ds1(2 * i + s)], base + 2 * i + s)
            base = st["ret_out"][0]
            with sp.Fori(0, KC) as i:
                for s in range(2):
                    load(s, FULL, a["w_ret_out"][ds1(2 * i + s)], base + 2 * i + s)
            ffn(1)
            for i in range(4):
                sp.wait_ge(h_ready, 3 * KC + 4 * i + 4)
                sp.dma_start(out[:, 4 * i:4 * i + 4, :], h[:, 4 * i:4 * i + 4, META:T]).then_inc(out_done, 16)
            sp.wait_ge(out_done, 4 * 16)

        CONSTS0 = 6 * 16
        CONSTS1 = 2 * 16

        FROM = [0, 0, 0, 0, 0, META, META, META]

        @block.tensor
        def _(pe):
            def mm(o, lhs, rhs, start, stop):
                return nc.tensor.matmul(o, lhs, rhs, start=start, stop=stop)

            def multiply(o, slot, w0, n, xh, xl, start=True, stop=True, before=None, behind=None, piece=None):
                for k in range(n):
                    if piece is not None and w0 + k == 8:
                        pe.wait_ge(lo_ready, 2 * piece + 2)
                    wh = w_hi[:, slot, (w0 + k) * P:(w0 + k + 1) * P]
                    wl = w_lo[:, slot, (w0 + k) * P:(w0 + k + 1) * P]
                    if before:
                        before(k)
                    mm(o, wh, xh(k), start and k == 0, False)
                    mm(o, wh, xl(k), False, False)
                    last = mm(o, wl, xh(k), False, stop and k == n - 1)
                    if piece is not None and w0 + k == 7:
                        last.then_inc(products, 1)
                    if behind:
                        behind(k)
                return last

            def open_tile(piece, tile):
                pe.wait_ge(lo_ready, 2 * piece + 1)
                if not (isinstance(tile, int) and tile < 2):
                    pe.wait_ge(drained, tile - 1)

            def sum_of(norm, k, slot):
                t0 = FROM[norm]
                pe.wait_ge(squared, KC * norm + k + 1)
                first = isinstance(k, int) and k == 0
                if first and norm:
                    pe.wait_ge(r_ready, norm)
                mm(ps[:, BK_SUM, t0:T], ones[:], sq[:, slot, t0:T], first,
                   isinstance(k, int) and k == KC - 1).then_inc(summed, 1)

            def fresh_pair(base, tile0, norm, t0):
                behind = 5 if norm else 10
                pe.wait_ge(lo_ready, 2 * base + 1)
                for k in range(KC + behind):
                    if k == behind:
                        pe.wait_ge(lo_ready, 2 * (base + 1) + 1)
                    if k == 8:
                        pe.wait_ge(lo_ready, 2 * base + 2)
                    if k == behind + 8:
                        pe.wait_ge(lo_ready, 2 * (base + 1) + 2)
                    if k < KC:
                        sum_of(norm, k, k % 2)
                        pe.wait_ge(x_lo_ready, KC * (norm // 2) + k + 1)
                        last = multiply(ps[:, BK_0, t0:T], 0, k, 1, lambda j: x_hi[:, k, t0:T],
                                        lambda j: x_lo[:, k, t0:T], k == 0, k == KC - 1)
                        if k == KC - 1:
                            last.then_inc(products, 2)
                    if k >= behind:
                        j = k - behind
                        last = multiply(ps[:, BK_1, t0:T], 1, j, 1, lambda _: x_hi[:, j, t0:T],
                                        lambda _: x_lo[:, j, t0:T], j == 0, j == KC - 1)
                last.then_inc(products, 2)

            def from_x(stage, n_pairs, norm=None, t0=0):
                base, _, tile0 = st[stage]

                def xh(k):
                    return x_hi[:, k, t0:T]

                def xl(k):
                    return x_lo[:, k, t0:T]

                if norm is None:
                    for s in range(2):
                        open_tile(base + s, tile0 + s)
                        multiply(ps[:, s, t0:T], s, 0, KC, xh, xl, piece=base + s).then_inc(products, 1)
                else:
                    fresh_pair(base, tile0, norm, t0)
                start = 1
                if norm is not None:
                    start = 2
                    if norm:
                        pe.wait_ge(drained, tile0)
                    for s in range(2, 4):
                        pe.wait_ge(lo_ready, 2 * (base + s) + 1)
                        multiply(ps[:, s % 2, t0:T], s % 2, 0, KC, xh, xl, piece=base + s).then_inc(products, 1)
                with pe.Fori(start, n_pairs) as i:
                    for s in range(2):
                        open_tile(base + 2 * i + s, tile0 + 2 * i + s)
                        multiply(ps[:, s, t0:T], s, 0, KC, xh, xl, piece=base + 2 * i + s).then_inc(products, 1)

            def out_proj(stage, n_sub, n_chunks, width, src_hi, src_lo, t0, norm, ready):
                base, _, tile0 = st[stage]

                def tile(i, s, fresh):
                    for sub in range(n_sub):
                        slot = (n_sub * s + sub) % 2
                        if sub == 0:
                            open_tile(base + n_sub * (2 * i + s), tile0 + 2 * i + s)
                        else:
                            pe.wait_ge(lo_ready, 2 * (base + n_sub * (2 * i + s) + sub) + 1)
                        multiply(ps[:, s, t0:T], slot, 0, n_chunks,
                                 lambda k: src_hi(sub * n_chunks + k), lambda k: src_lo(sub * n_chunks + k),
                                 sub == 0, sub == n_sub - 1,
                                 before=(lambda k: ready(sub * n_chunks + k)) if fresh else None,
                                 piece=base + n_sub * (2 * i + s) + sub).then_inc(products, 1)

                for s in range(2):
                    tile(0, s, s == 0)
                with pe.Fori(1, 8) as i:
                    for s in range(2):
                        tile(i, s, False)
                if norm is not None:
                    pe.wait_ge(summed, KC * (norm + 1))
                    pe.wait_ge(r_ready, norm)
                    mm(ps[:, BK_SUM, t0:T], ones[:], sq_sum[:, t0:T], True, True).then_inc(totalled, 1)

            pe.wait_ge(ones_in, 16)
            from_x("latent", 4, norm=0)
            pe.wait_ge(const_in, CONSTS0)
            pe.wait_ge(cleared, 1)

            def part(i, s, k0, k1):
                piece, _, tile, _ = head_at(i)
                if k0 == 0:
                    open_tile(piece + s, tile + s)
                last = multiply(ps[:, s % 2, 0:T], s % 2, k0, k1 - k0, lambda k: x_hi[:, k0 + k],
                                lambda k: x_lo[:, k0 + k], k0 == 0, k1 == KC, piece=piece + s)
                if k1 == KC:
                    last.then_inc(products, 1)

            def index_pair(i, slot):
                if not isinstance(i, int) or i not in (1, 2) or (i == 2 and slot >= 8):
                    return
                for c in range(2 * slot, 2 * slot + 2):
                    c += 2 * IDX_HEADS * (i - 1)
                    b, n_head = divmod(c, IDX_HEADS)
                    q0, n = BLK[b]
                    half = IDX_DIM * (n_head % 2)
                    if c >= 2:
                        pe.wait_ge(relued, c - 1)
                    mm(ps[0:n, BK_D0 + c % 2, 0:ROW[b][1]], q_index[half:half + IDX_DIM, n_head // 2, q0:q0 + n],
                       kidx[half:half + IDX_DIM, 0:ROW[b][1]], True, True).then_inc(dots, 1)

            def dsa_q(i):
                piece, _, tile, _ = dsa_at(i)
                open_tile(piece, tile)
                multiply(ps[:, 0, 0:T], 0, 0, 4, lambda k: cq_hi[:, k], lambda k: cq_lo[:, k]).then_inc(products, 1)

            def dsa_kv(i):
                piece, _, tile, _ = dsa_at(i)
                open_tile(piece + 1, tile + 1)
                multiply(ps[:, 1, 0:T], 1, 0, 2, lambda k: ckv_hi[:, k, 0:T], lambda k: ckv_lo[:, k, 0:T]
                         ).then_inc(products, 1)
                for b in range(3):
                    o = ps[:, BK_D0, b * P:(b + 1) * P]
                    for k in range(2):
                        xh, xl = ckv_hi[:, k, b * P:(b + 1) * P], ckv_lo[:, k, b * P:(b + 1) * P]
                        wh, wl = w_hi[:, 1, (2 + k) * P:(3 + k) * P], w_lo[:, 1, (2 + k) * P:(3 + k) * P]
                        mm(o, xh, wh, k == 0, False)
                        mm(o, xl, wh, False, False)
                        last = mm(o, xh, wl, False, k == 1)
                last.then_inc(products, 1)

            def dsa_logits(i):
                pe.wait_ge(drained, dsa_at(i)[2] + 2)
                pe.wait_ge(DA.sem, DA.after("values", i))
                for b, (q0, n) in enumerate(BLK):
                    keys = ROW[b][1]
                    o = ps[0:n, BK_D0, 128 * b:128 * b + keys] if b < 2 else ps[0:n, BK_D1, 0:keys]
                    last = mm(o, q_h[:, q0:q0 + n], k_h[:, 0:keys], True, True)
                last.then_inc(DP.sem, 1)

            def dsa_turn(i):
                pe.wait_ge(DA.sem, DA.after("probs", i))
                for kb, (c0, qf, nq) in enumerate(TROW):
                    k0, nk = BLK[kb]
                    for b, (q0, n) in enumerate(BLK):
                        if b >= kb:
                            c = c0 + q0 - qf
                            last = nc.tensor.transpose(ps[0:nk, BK_D0, c:c + n],
                                                       dsa_s[0:n, ROW[b][0] + k0:ROW[b][0] + k0 + nk],
                                                       ident[0:n, 0:n])
                last.then_inc(DP.sem, 1)

            def dsa_attend(i):
                pe.wait_ge(DA.sem, DA.after("turned", i))
                for kb, (c0, qf, nq) in enumerate(TROW):
                    nk = BLK[kb][1]
                    last = mm(ps[:, BK_D1, qf:qf + nq], v_h[0:nk, kb, :], p_t[0:nk, c0:c0 + nq], kb == 0, kb == 2)
                last.then_inc(DP.sem, 1)

            def dsa_end(i):
                pe.wait_ge(DV.sem, DV.after("y_lo", i))

            def c(n):
                return slice(n * CH, (n + 1) * CH)

            def out_sum(i):
                pe.wait_ge(FA.sem, FA.after("o", i))
                mm(ps[:, BK_3, 0:T], ones[:], o_sq, True, True).then_inc(FP.sem, 1)

            def gdn_sums(i):
                pe.wait_ge(GA.sem, GA.after("squared", i))
                mm(ps[:, BK_0, 0:T], ones[:], kq[:, 2, 0:T], True, True)
                mm(ps[:, BK_1, 0:T], ones[:], kq[:, 3, 0:T], True, True).then_inc(GP.sem, 1)

            def gdn_spread(i, f):
                if f is not None:
                    pe.wait_ge(FA.sem, FA.after("ln", f))
                pe.wait_ge(GV.sem, GV.after("select", i))
                mm(ps[:, BK_2, 0:LP], ones[0:HEADS, :], gsel[:, 0, :], True, True)
                mm(ps[:, BK_3, 0:LP], ones[0:HEADS, :], gsel[:, 1, :], True, True).then_inc(GP.sem, 1)

            def gdn_scores(i):
                pe.wait_ge(GV.sem, GV.after("kb", i))
                for n in range(NCH):
                    mm(ps[0:CH, BK_0, c(n)], kq[:, 0, c(n)], kq[:, 2, c(n)], True, True)
                for n in range(NCH):
                    last = mm(ps[0:CH, BK_1, c(n)], kq[:, 0, c(n)], kq[:, 1, c(n)], True, True)
                last.then_inc(GP.sem, 1)

            def gdn_turn(i):
                pe.wait_ge(GV.sem, GV.after("arg", i))
                pe.wait_ge(GA.sem, GA.after("decayed", i))
                pe.wait_ge(CA.sem, CA.after("silu2", i))
                for n in range(NCH):
                    nc.tensor.transpose(ps[0:CH, BK_2, n * P:(n + 1) * P], kq[:, 0, c(n)], ident[:])
                for n in range(NCH):
                    last = nc.tensor.transpose(ps[0:CH, BK_3, n * P:(n + 1) * P], qkv[:, 2, c(n)], ident[:])
                last.then_inc(GP.sem, 1)

            def gdn_tm0(i):
                pe.wait_ge(GV.sem, GV.after("tt0", i))
                for n in range(NCH):
                    last = nc.tensor.transpose(ps[0:CH, BK_0, c(n)], tt[:, n], ident[0:CH, 0:CH])
                last.then_inc(GP.sem, 1)

            def gdn_y(i, l):
                pe.wait_ge(GG.sem, GG.after(f"lev{l}", i))
                if l == 1:
                    pe.wait_ge(GA.sem, GA.after("tm0", i))
                else:
                    pe.wait_ge(GV.sem, GV.after(f"tm{l - 1}", i))
                for n in range(NCH):
                    last = mm(ps[0:CH, BK_1, c(n)], at_l[:, n], tm[:, n], True, True)
                last.then_inc(GP.sem, 1)

            def gdn_z(i, l):
                pe.wait_ge(GA.sem, GA.after(f"y{l}", i))
                pe.wait_ge(GV.sem, GV.after(f"tt{l - 1}" if l > 1 else "rows", i))
                if l < LEVELS - 1:
                    for n in range(NCH):
                        last = mm(ps[0:CH, BK_0, c(n)], tt[:, n], ym[:, n], True, True)
                    last.then_inc(GP.sem, 1)
                for n in range(NCH):
                    last = mm(ps[0:CH, BK_2, c(n)], ym[:, n], tt[:, n], True, True)
                last.then_inc(GP.sem, 1)

            def gdn_w(i):
                pe.wait_ge(GV.sem, GV.after(f"tt{LEVELS - 1}", i))
                for n in range(NCH):
                    last = mm(ps[:, BK_1, c(n)], kbg[:, n], tt[:, n], True, True)
                last.then_inc(GP.sem, 1)

            def gdn_v(i, n):
                if n:
                    pe.wait_ge(GV.sem, GV.after(f"s{n - 1}", i))
                mv = mm(ps[0:CH, BK_3, n * P:(n + 1) * P], tt[:, n], vb[:, n], True, n == 0)
                if n:
                    if n == 1:
                        pe.wait_ge(GA.sem, GA.after("w", i))
                    mv = mm(ps[0:CH, BK_3, n * P:(n + 1) * P], wneg[:, c(n)], state[:], False, True)
                mv.then_inc(GP.sem, 1)

            def gdn_o(i, n):
                pe.wait_ge(GA.sem, GA.after(f"vn{n}", i))
                if n:
                    mm(ps[:, BK_0, c(n)], state[:], kq[:, 3, c(n)], True, False)
                if n < NCH - 1:
                    mm(ps[:, BK_2, 0:P], kd[:, n], v_new[:, n], True, True).then_inc(GP.sem, 1)
                last = mm(ps[:, BK_0, c(n)], v_new[:, n], qk[:, n], n == 0, True)
                if n == NCH - 1:
                    last.then_inc(GP.sem, 1)

            def mixer_body(i, g, f, d):
                if d is not None:
                    dsa_q(d)
                if f is not None:
                    out_sum(f)
                if d is not None:
                    dsa_kv(d)
                if g is not None:
                    gdn_sums(g)
                    gdn_spread(g, f)
                index_pair(i, 0)
                part(i, 0, 0, 4)
                index_pair(i, 1)
                part(i, 0, 4, 6)
                if d is not None:
                    dsa_logits(d)
                part(i, 0, 6, 9)
                if g is not None:
                    gdn_scores(g)
                index_pair(i, 2)
                part(i, 0, 9, 12)
                if g is not None:
                    gdn_turn(g)
                index_pair(i, 3)
                part(i, 0, 12, 16)
                part(i, 1, 0, 2)
                if g is not None:
                    gdn_tm0(g)
                index_pair(i, 4)
                part(i, 1, 2, 4)
                if d is not None:
                    dsa_turn(d)
                part(i, 1, 4, 6)
                for l in range(1, 4):
                    if g is not None:
                        gdn_y(g, l)
                    if l < 3:
                        part(i, 1, 3 + 3 * l, 5 + 3 * l)
                    else:
                        part(i, 1, 12, 14)
                    if l == 1 and d is not None:
                        dsa_attend(d)
                    if g is not None:
                        gdn_z(g, l)
                    index_pair(i, 4 + l)
                    part(i, 1, *[(8, 9), (11, 12), (14, 16)][l - 1])
                for l in range(4, LEVELS):
                    if g is not None:
                        gdn_y(g, l)
                    part(i, 2, 4 * l - 16, 4 * l - 14)
                    if g is not None:
                        gdn_z(g, l)
                    index_pair(i, 4 + l)
                    part(i, 2, 4 * l - 14, 4 * l - 12)
                if g is not None:
                    gdn_w(g)
                index_pair(i, 11)
                part(i, 2, 12, 14)
                if g is not None:
                    gdn_v(g, 0)
                part(i, 2, 14, 16)
                if g is not None:
                    gdn_o(g, 0)
                index_pair(i, 12)
                part(i, 3, 0, 3)
                if g is not None:
                    gdn_v(g, 1)
                index_pair(i, 13)
                part(i, 3, 3, 6)
                if g is not None:
                    gdn_o(g, 1)
                index_pair(i, 14)
                part(i, 3, 6, 9)
                if g is not None:
                    gdn_v(g, 2)
                index_pair(i, 15)
                part(i, 3, 9, 12)
                if g is not None:
                    gdn_o(g, 2)
                part(i, 3, 12, 16)
                if d is not None:
                    dsa_end(d)

            part(0, 0, 0, 4)
            pe.wait_ge(LA.sem, LA.after("squared"))
            for k in range(4):
                mm(ps[:, BK_D1, 0:T], ones[:], q_index[:, k], k == 0, k == 3)
            for k in range(2):
                mm(ps[:, BK_0, 0:T], ones[:], q_index[:, 4 + k], k == 0, k == 1)
            mm(ps[:, BK_1, 0:T], ones[:], q_index[:, 6], True, True).then_inc(LP_.sem, 1)
            for b, (q0, n) in enumerate(BLK):
                last = nc.tensor.transpose(ps[0:n, BK_3, 16 * b:16 * b + 16], lat[0:16, 7, q0:q0 + n],
                                           ident[0:16, 0:16])
            last.then_inc(LP_.sem, 1)
            part(0, 0, 4, 16)
            part(0, 1, 0, 16)
            part(0, 2, 0, 16)
            part(0, 3, 0, 16)

            pe.wait_ge(LV.sem, LV.after("lo"))
            for t in range(8):
                open_tile(INDEX_Q[0] + t // 4, INDEX_Q[2] + t)
                if t % 4 == 2:
                    pe.wait_ge(lo_ready, 2 * (INDEX_Q[0] + t // 4) + 2)
                multiply(ps[:, t % 2, 0:T], t // 4, 4 * (t % 4), 4, lambda k: cq_hi[:, k], lambda k: cq_lo[:, k]
                         ).then_inc(products, 1)
            pe.wait_ge(LV.sem, LV.after("scan2"))
            for w in range(2):
                for n in range(NCH):
                    c0 = (w * NCH + n) * HEADS
                    last = nc.tensor.transpose(ps[0:CH, BK_2, c0:c0 + HEADS], gb8[:, w, n * CH:(n + 1) * CH],
                                               ident[0:HEADS, 0:HEADS])
            last.then_inc(LP_.sem, 1)
            pe.wait_ge(drained, INDEX_Q[2] + 8)
            pe.wait_ge(LV.sem, LV.after("cols01"))

            mixer_body(1, 0, None, None)
            mixer_body(2, 1, 0, None)
            pe.wait_ge(relued, 3 * IDX_HEADS)
            with pe.Fori(0, HEADS - LAG) as i:
                mixer_body(i + 3, i + 2, i + 1, i)

            g, d = HEADS - 1, HEADS - LAG
            dsa_q(d)
            out_sum(g - 1)
            dsa_kv(d)
            gdn_sums(g)
            gdn_spread(g, g - 1)
            dsa_logits(d)
            gdn_scores(g)
            gdn_turn(g)
            gdn_tm0(g)
            dsa_turn(d)
            gdn_y(g, 1)
            dsa_attend(d)
            gdn_z(g, 1)
            dsa_end(d)
            dsa_q(d + 1)
            gdn_y(g, 2)
            dsa_kv(d + 1)
            gdn_z(g, 2)
            gdn_y(g, 3)
            dsa_logits(d + 1)
            gdn_z(g, 3)
            gdn_y(g, 4)
            gdn_z(g, 4)
            gdn_y(g, 5)
            dsa_turn(d + 1)
            gdn_z(g, 5)
            gdn_y(g, 6)
            dsa_attend(d + 1)
            gdn_z(g, 6)
            dsa_end(d + 1)
            dsa_q(d + 2)
            gdn_w(g)
            gdn_v(g, 0)
            dsa_kv(d + 2)
            gdn_o(g, 0)
            gdn_v(g, 1)
            dsa_logits(d + 2)
            gdn_o(g, 1)
            gdn_v(g, 2)
            gdn_o(g, 2)
            dsa_turn(d + 2)
            out_sum(g)
            dsa_attend(d + 2)

            def ready_y(k):
                if k == 0:
                    pe.wait_ge(DV.sem, DV.after("y_lo", HEADS - 1))
                if k == HEADS:
                    pe.wait_ge(FV.sem, FV.after("y_lo", HEADS - 1))

            out_proj("mix_out", 1, KC, FULL, lambda k: y_hi[:, k], lambda k: y_lo[:, k], 0, 1, ready_y)

            def ffn(layer, norm):
                t0 = FROM[norm]
                w = T - t0
                for half in range(2):
                    n = 2 * layer + half
                    from_x(f"up{n}", HALF, norm=norm if half == 0 else None, t0=t0)
                    out_proj(f"down{n}", 2, SUB, FFN_W,
                             lambda k: mid_hi[:, k * w:(k + 1) * w], lambda k: mid_lo[:, k * w:(k + 1) * w], t0,
                             norm + 1 if half else None,
                             lambda k: pe.wait_ge(mid_lo_ready, HALF * n + k + 1))

            ffn(0, 2)

            base, _, tile0 = st["ret_in"]

            def ret_tile(i, s, t0=0):
                if isinstance(i, int) and s < 4:
                    pe.wait_ge(lo_ready, 2 * (base + s) + 1)
                else:
                    open_tile(base + 12 * i + s, tile0 + 12 * i + s)
                multiply(ps[:, s % 2, t0:T], s % 2, 0, KC, lambda k: x_hi[:, k, t0:T], lambda k: x_lo[:, k, t0:T],
                         piece=base + 12 * i + s).then_inc(products, 1)

            def turn_v(i, j):
                pe.wait_ge(drained, tile0 + 12 * i + 4 + j + 1)
                if j:
                    pe.wait_ge(RA.sem, RA.after(f"vr{j - 1}", i))
                for b, (q0, n) in enumerate(BLK):
                    last = nc.tensor.transpose(ps[0:n, BK_D1, b * P:(b + 1) * P], v_t[:, q0:q0 + n], ident[:])
                last.then_inc(RP.sem, 1)

            def ret_round(i, norm=None):
                if norm is not None:
                    fresh_pair(base, tile0, norm, 0)
                for s in range(2 if norm is not None else 0, 4):
                    ret_tile(i, s, META if s < 2 else 0)
                ret_tile(i, 4)
                ret_tile(i, 5)
                turn_v(i, 0)
                ret_tile(i, 6)
                turn_v(i, 1)
                ret_tile(i, 7)
                turn_v(i, 2)
                ret_tile(i, 8, META)
                turn_v(i, 3)
                pe.wait_ge(RG.sem, RG.after("k", i))
                for kb, (c0, q0, nq) in enumerate(RROW):
                    k0, nk = BLK[kb]
                    for c in range(2):
                        last = mm(ps[0:nk, BK_D0, c0:c0 + nq], k_rot[:, c, k0:k0 + nk], q_rot[:, c, q0:q0 + nq],
                                  c == 0, c == 1)
                last.then_inc(RP.sem, 1)
                ret_tile(i, 9, META)
                pe.wait_ge(RV.sem, RV.after("s2", i))
                pe.wait_ge(RA.sem, RA.after("vr3", i))
                for j in range(4):
                    for kb, (c0, q0, nq) in enumerate(RROW):
                        nk = BLK[kb][1]
                        c = SEQ * (j % 2) + q0
                        last = mm(ps[:, BK_0 + j // 2, c:c + nq], v_rows[0:nk, kb, j * P:(j + 1) * P],
                                  ret_s[0:nk, c0:c0 + nq], kb == 0, kb == 2)
                last.then_inc(RP.sem, 1)
                ret_tile(i, 10, META)
                pe.wait_ge(RA.sem, RA.after("osq", i))
                for j in range(4):
                    last = mm(ps[:, BK_2, 0:SEQ], ones[:], ret_sq[:, j], j == 0, j == 3)
                last.then_inc(RP.sem, 1)
                ret_tile(i, 11, META)

            ret_round(0, 4)
            with pe.Fori(1, HEADS) as i:
                ret_round(i)

            def ready_ret(k):
                if k == 0:
                    pe.wait_ge(RV.sem, RV.after("y_lo", HEADS - 1))

            out_proj("ret_out", 2, KC, FULL, lambda k: mid_hi[:, k * SEQ:(k + 1) * SEQ],
                     lambda k: mid_lo[:, k * SEQ:(k + 1) * SEQ], META, 5, ready_ret)
            ffn(1, 6)

        @block.scalar
        def _(act):
            def split_hi(nth, width, piece, signals, step=1):
                act.wait_ge(piece_in[piece % 2], 16 * nth)
                for b, (cut, count) in enumerate(halves(width)):
                    if signals is not None:
                        act.wait_ge(products, signals + step * b)
                    nc.scalar.activation(w_hi[:, piece % 2, cut], raw[:, piece % 2, cut],
                                         ACT.Copy).then_inc(hi_ready, count)

            def split_next(stage, i, q, per_round, width):
                base, sig, _ = st[stage]
                split_hi(base // 2 + per_round // 2 * i + (q + 1) // 2 + 1, width, q + 1,
                         sig + 2 * per_round * i + 2 * q - 1)

            def apart():
                act.wait_ge(cleared, 1)

            def square(norm, k, slot, src, src_ready, ready_at):
                t0 = FROM[norm]
                act.wait_ge(src_ready, ready_at)
                n = KC * norm + k
                if not (isinstance(n, int) and n < 2):
                    act.wait_ge(summed, n - 1)
                apart()
                nc.scalar.activation(sq[:, slot, t0:T], src[:, ds1(k), t0:T], ACT.Square).then_inc(squared, 1)

            def take_root(norm, dst):
                t0 = FROM[norm]
                if norm % 2:
                    act.wait_ge(totalled, norm // 2 + 1)
                else:
                    act.wait_ge(summed, KC * (norm + 1))
                    if norm:
                        act.wait_ge(x_lo_ready, KC * (norm // 2))
                nc.scalar.activation(dst[:, t0:T], ps[:, BK_SUM, t0:T], ACT.Sqrt, scale=1.0 / D, bias=eps_col[:, 0:1]
                                     ).then_inc(rooted, 1)

            def table(func):
                nc.scalar.activation(scratch[:, 1:2], scratch[:, 0:1], func)

            def fill_x(norm, loaded, after=None):
                t0 = FROM[norm]

                def chunk(k, slot):
                    n = KC * norm + k
                    if not loaded:
                        act.wait_ge(h_ready, KC * (norm // 2 - 1) + k + 1)
                    if not (isinstance(n, int) and n < 2):
                        act.wait_ge(summed, n - 1)
                    apart()
                    nc.scalar.activation(x_hi[:, ds1(k), t0:T], h[:, ds1(k), t0:T], ACT.Copy,
                                         scale=gains[:, norm, ds1(k)]).then_inc(x_hi_ready, 1)
                    nc.scalar.activation(sq[:, slot, t0:T], h[:, ds1(k), t0:T], ACT.Square).then_inc(squared, 1)

                if loaded:
                    for k in range(KC):
                        if k % 4 == 0:
                            act.wait_ge(h_in[k // 4], 16)
                        if k == 8:
                            split_hi(1, FULL, 1, None)
                        chunk(k, k % 2)
                    after()
                else:
                    with act.Fori(0, KC // 2) as i:
                        for s in range(2):
                            chunk(2 * i + s, s)
                    after()
                take_root(norm, r_pre)

            def out_proj(stage, n_sub, width, next_width, norm, following=None):
                tile0 = st[stage][2]

                def body(i, last):
                    for s in range(2):
                        for sub in range(n_sub):
                            q = n_sub * s + sub
                            w = next_width if last and q == 2 * n_sub - 1 else width
                            if w:
                                split_next(stage, i, q, 2 * n_sub, w)
                        if norm is not None:
                            if last and s:
                                table(ACT.Sqrt)
                            square(norm, 2 * i + s, s, u, drained, tile0 + 2 * i + s + 1)
                rounds(act, 8, body)
                if norm is not None:
                    if following:
                        split_next(following, 0, 0, 4, FULL)
                    take_root(norm, r_post)

            def split_head(i, s, parts=(0, 1)):
                piece, sig, _, loads = head_at(i)
                w = 4 * P if s == 4 and not (isinstance(i, int) and i < LAG - 1) else FULL
                for p in parts:
                    if p >= len(halves(w)):
                        continue
                    cut, count = halves(w)[p]
                    if p == 0:
                        act.wait_ge(piece_in[s % 2], 16 * (loads + s // 2 + 1))
                    if s == 1 and not (isinstance(i, int) and i < LAG):
                        act.wait_ge(products, sig)
                    else:
                        act.wait_ge(products, sig + 2 * s - 3 + p)
                    nc.scalar.activation(w_hi[:, s % 2, cut], raw[:, s % 2, cut], ACT.Copy).then_inc(hi_ready, count)

            def split_dsa(i, s, width):
                piece, sig, _, loads = dsa_at(i)
                if s == 2:
                    done = sig + 1
                else:
                    done = sig if isinstance(i, int) and i > HEADS - LAG else sig - 1
                split_hi(loads + s // 2 + 1, width, s, done, 0)

            act.wait_ge(gains_in, 16)
            act.wait_ge(cleared, 1)
            split_hi(1, FULL, 0, None)
            fill_x(0, True, lambda: split_next("latent", 0, 1, 2, FULL))
            for q in range(2, 8):
                i, s = divmod(q, 2)
                split_next("latent", i, s, 2, FULL)

            split_head(0, 1)
            act.wait_ge(const_in, CONSTS0)
            act.wait_ge(drained, 8)
            nc.scalar.activation(q_index[:, 0:7], lat[:, 0:7], ACT.Square).then_inc(LA.sem, 1)
            act.wait_ge(LP_.sem, LP_.after("summed"))
            for r, (bank, width) in enumerate(((BK_D1, 4 * P), (BK_0, 2 * P), (BK_1, P))):
                last = nc.scalar.activation(kq[:, 1 + r, 0:T], ps[:, bank, 0:T], ACT.Sqrt, scale=1.0 / width,
                                            bias=eps_col[:, 0:1])
            last.then_inc(LA.sem, 1)
            split_head(0, 2)
            act.wait_ge(LV.sem, LV.after("norm_q"))
            nc.scalar.activation(cq_hi[:], lat[:, 0:4], ACT.Copy).then_inc(LA.sem, 1)
            act.wait_ge(LV.sem, LV.after("norm_kv"))
            nc.scalar.activation(ckv_hi[:, :, 0:T], lat[:, 4:6], ACT.Copy).then_inc(LA.sem, 1)
            split_head(0, 3)
            act.wait_ge(LV.sem, LV.after("shifted"))
            nc.scalar.activation(gb8[:, 1, 0:T], gb8[:, 1, 0:T], ACT.Exp, scale=-1.0).then_inc(LA.sem, 1)
            act.wait_ge(LV.sem, LV.after("abs"))
            nc.scalar.activation(gsel[:, 1, 0:T], gsel[:, 1, 0:T], ACT.Exp).then_inc(LA.sem, 1)
            act.wait_ge(LA.sem, LA.after("exp"))
            nc.scalar.activation(gsel[:, 1, 0:T], gsel[:, 1, 0:T], ACT.Ln, bias=eps_col[0:HEADS, 1:2]).then_inc(LA.sem, 1)
            nc.scalar.activation(decay8[:, 2:3], decay8[:, 0:1], ACT.Exp).then_inc(LA.sem, 1)

            def index_pair(i, slot):
                if not isinstance(i, int) or i not in (1, 2) or (i == 2 and slot >= 8):
                    return
                for c in range(2 * slot, 2 * slot + 2):
                    c += 2 * IDX_HEADS * (i - 1)
                    b = c // IDX_HEADS
                    n, keys, at0 = BLK[b][1], ROW[b][1], T * (c % 2)
                    act.wait_ge(dots, c + 1)
                    if c >= 2:
                        act.wait_ge(scored, c - 1)
                    nc.scalar.activation(dsa_s[0:n, at0:at0 + keys], ps[0:n, BK_D0 + c % 2, 0:keys],
                                         ACT.Relu).then_inc(relued, 1)

            def silu(i, s, g):
                act.wait_ge(CV.sem, CV.after(f"t{s}3", i))
                if g is not None:
                    if s < 2:
                        act.wait_ge(GV.sem, GV.after("kq", g))
                    else:
                        act.wait_ge(GP.sem, GP.after("turned", g))
                nc.scalar.activation(qkv[:, s, 0:T], conv_acc[:, s], ACT.Silu).then_inc(CA.sem, 1)

            def gate_of(i, f):
                act.wait_ge(drained, head_at(i)[2] + 4)
                if f is not None:
                    act.wait_ge(FV.sem, FV.after("om1", f))
                nc.scalar.activation(gate[:], r_post[:], ACT.Silu).then_inc(CA.sem, 1)

            def dsa_values(i):
                act.wait_ge(products, dsa_at(i)[1] + 3)
                nc.scalar.activation(v_h[:].rearrange("p b t -> p (b t)"), ps[:, BK_D0, 0:3 * P], ACT.Copy
                                     ).then_inc(DA.sem, 1)

            def dsa_exp(i):
                act.wait_ge(DV.sem, DV.after("maxed", i))
                for b, (q0, n) in enumerate(BLK):
                    c0, keys = ROW[b]
                    last = nc.scalar.activation(dsa_s[0:n, c0:c0 + keys], dsa_s[0:n, c0:c0 + keys], ACT.Exp,
                                                bias=mx[0:n, b:b + 1], accum_out=rs[0:n, b:b + 1])
                last.then_inc(DA.sem, 1)

            def dsa_probs(i):
                act.wait_ge(DV.sem, DV.after("recips", i))
                for b, (q0, n) in enumerate(BLK):
                    c0, keys = ROW[b]
                    last = nc.scalar.activation(dsa_s[0:n, c0:c0 + keys], dsa_s[0:n, c0:c0 + keys], ACT.Copy,
                                                scale=rinv[0:n, b:b + 1])
                last.then_inc(DA.sem, 1)

            def dsa_turned(i):
                act.wait_ge(DP.sem, DP.after("turned", i))
                nc.scalar.activation(p_t[:, 0:416], ps[:, BK_D0, 0:416], ACT.Copy)
                nc.scalar.activation(p_t[0:16, 416:432], ps[0:16, BK_D0, 416:432], ACT.Copy).then_inc(DA.sem, 1)

            def dsa_y(i):
                act.wait_ge(DP.sem, DP.after("attended", i))
                apart()
                nc.scalar.activation(y_hi[:, ds1(i), :], ps[:, BK_D1, 0:T], ACT.Copy).then_inc(DA.sem, 1)

            def gdn_square(i):
                nc.scalar.activation(kq[:, 2:4, 0:T], qkv[:, 0:2, 0:T], ACT.Square).then_inc(GA.sem, 1)

            def gdn_ln(i):
                act.wait_ge(GP.sem, GP.after("sums", i))
                nc.scalar.activation(kq[:, 2:4, 0:T], ps[:, BK_0:BK_1 + 1, 0:T], ACT.Ln, bias=eps_col[:, 0:1]
                                     ).then_inc(GA.sem, 1)

            def gdn_rnorm(i):
                act.wait_ge(GA.sem, GA.after("ln", i))
                nc.scalar.activation(kq[:, 2:4, 0:T], kq[:, 2:4, 0:T], ACT.Exp, scale=-0.5).then_inc(GA.sem, 1)

            def gdn_decayed(i):
                act.wait_ge(GP.sem, GP.after("spread", i))
                nc.scalar.activation(dec[:], ps[:, BK_2, 0:LP], ACT.Exp).then_inc(GA.sem, 1)

            def gdn_decmat(i):
                act.wait_ge(GV.sem, GV.after("arg", i))
                nc.scalar.activation(kd_last[:], kd_last[:], ACT.Exp)
                nc.scalar.activation(at_l, at_l, ACT.Exp).then_inc(GA.sem, 1)

            def gdn_tm0(i):
                act.wait_ge(GP.sem, GP.after("tm0", i))
                nc.scalar.activation(tm.rearrange("p n t -> p (n t)"), ps[0:CH, BK_0, 0:LP], ACT.Copy
                                     ).then_inc(GA.sem, 1)

            def gdn_y(i, l):
                act.wait_ge(GP.sem, GP.after(f"y{l}", i))
                nc.scalar.activation(ym.rearrange("p n t -> p (n t)"), ps[0:CH, BK_1, 0:LP], ACT.Copy
                                     ).then_inc(GA.sem, 1)

            def gdn_w(i):
                act.wait_ge(GP.sem, GP.after("w", i))
                nc.scalar.activation(wneg, ps[:, BK_1, 0:LP], ACT.Copy, scale=-1.0).then_inc(GA.sem, 1)

            def gdn_v(i, n):
                act.wait_ge(GP.sem, GP.after(f"v{n}", i))
                nc.scalar.activation(v_new[:, n], ps[0:CH, BK_3, n * P:(n + 1) * P], ACT.Copy).then_inc(GA.sem, 1)

            def out_take(i):
                act.wait_ge(GP.sem, GP.after("o2", i))
                if not (isinstance(i, int) and i == 0):
                    act.wait_ge(FV.sem, FV.after("y_lo", i - 1))
                nc.scalar.activation(o_m, ps[:, BK_0, 0:T], ACT.Copy, scale=lat_gain[:, 7:8])
                nc.scalar.activation(o_sq, ps[:, BK_0, 0:T], ACT.Square).then_inc(FA.sem, 1)

            def out_ln(i):
                act.wait_ge(FP.sem, FP.after("osum", i))
                nc.scalar.activation(o_sq, ps[:, BK_3, 0:T], ACT.Ln, scale=1.0 / P, bias=eps_col[:, 0:1]
                                     ).then_inc(FA.sem, 1)

            def out_rnorm(i):
                act.wait_ge(FA.sem, FA.after("ln", i))
                nc.scalar.activation(o_sq, o_sq, ACT.Exp, scale=-0.5).then_inc(FA.sem, 1)

            def out_y(i):
                act.wait_ge(FV.sem, FV.after("om1", i))
                apart()
                nc.scalar.activation(y_hi[:, ds1(i + HEADS), :], o_m, ACT.Copy).then_inc(FA.sem, 1)

            def mixer_body(i, g, f, d):
                if d is not None:
                    split_dsa(d, 1, 4 * P)
                if g is not None:
                    gdn_square(g)
                if d is not None:
                    split_dsa(d, 2, FULL)
                if f is not None:
                    out_ln(f)
                if g is not None:
                    gdn_ln(g)
                if f is not None:
                    out_rnorm(f)
                if g is not None:
                    gdn_rnorm(g)
                if d is not None:
                    dsa_values(d)
                if g is not None:
                    gdn_decayed(g)
                split_head(i, 1, (0,))
                if f is not None:
                    out_y(f)
                index_pair(i, 0)
                if g is not None:
                    gdn_decmat(g)
                split_head(i, 1, (1,))
                index_pair(i, 1)
                if d is not None:
                    dsa_exp(d)
                index_pair(i, 2)
                if d is not None:
                    dsa_probs(d)
                index_pair(i, 3)
                if d is not None:
                    dsa_turned(d)
                if g is not None:
                    gdn_tm0(g)
                split_head(i, 2, (0,))
                index_pair(i, 4)
                for l in range(1, 4):
                    if g is not None:
                        gdn_y(g, l)
                    if l == 1:
                        if d is not None:
                            dsa_y(d)
                        split_head(i, 2, (1,))
                    index_pair(i, 4 + l)
                if g is not None:
                    gdn_y(g, 4)
                split_head(i, 3, (0,))
                index_pair(i, 8)
                if g is not None:
                    gdn_y(g, 5)
                split_head(i, 3, (1,))
                index_pair(i, 9)
                if g is not None:
                    gdn_y(g, 6)
                if g is not None:
                    gate_of(g, f)
                silu(i, 0, g)
                silu(i, 1, g)
                index_pair(i, 10)
                if g is not None:
                    gdn_w(g)
                index_pair(i, 11)
                if g is not None:
                    gdn_v(g, 0)
                index_pair(i, 12)
                split_head(i, 4, (0,))
                index_pair(i, 13)
                if g is not None:
                    gdn_v(g, 1)
                split_head(i, 4, (1,))
                index_pair(i, 14)
                index_pair(i, 15)
                if g is not None:
                    gdn_v(g, 2)
                    out_take(g)
                silu(i, 2, g)

            silu(0, 0, None)
            silu(0, 1, None)
            split_head(0, 4)
            silu(0, 2, None)
            split_hi(INDEX_Q[0] // 2 + 1, FULL, 1, INDEX_Q[1] - 1)
            split_hi(INDEX_Q[0] // 2 + 2, FULL, 0, INDEX_Q[1] + 2, 2)
            act.wait_ge(LV.sem, LV.after("cols01"))
            nc.scalar.activation(cols[:, 2], cols[:, 0], ACT.Exp).then_inc(LA.sem, 1)
            mixer_body(1, 0, None, None)
            mixer_body(2, 1, 0, None)
            with act.Fori(0, HEADS - LAG) as i:
                mixer_body(i + 3, i + 2, i + 1, i)

            g, d = HEADS - 1, HEADS - LAG
            split_dsa(d, 1, 4 * P)
            gdn_square(g)
            split_dsa(d, 2, 4 * P)
            out_ln(g - 1)
            gdn_ln(g)
            out_rnorm(g - 1)
            gdn_rnorm(g)
            dsa_values(d)
            gdn_decayed(g)
            gate_of(g, g - 1)
            out_y(g - 1)
            gdn_decmat(g)
            dsa_exp(d)
            dsa_probs(d)
            split_dsa(d + 1, 1, 4 * P)
            gdn_tm0(g)
            dsa_turned(d)
            gdn_y(g, 1)
            dsa_y(d)
            split_dsa(d + 1, 2, 4 * P)
            gdn_y(g, 2)
            dsa_values(d + 1)
            gdn_y(g, 3)
            split_dsa(d + 2, 1, 4 * P)
            dsa_exp(d + 1)
            gdn_y(g, 4)
            dsa_probs(d + 1)
            gdn_y(g, 5)
            dsa_turned(d + 1)
            gdn_y(g, 6)
            dsa_y(d + 1)
            split_dsa(d + 2, 2, FULL)
            gdn_w(g)
            gdn_v(g, 0)
            dsa_values(d + 2)
            gdn_v(g, 1)
            dsa_exp(d + 2)
            gdn_v(g, 2)
            out_take(g)
            dsa_probs(d + 2)
            dsa_turned(d + 2)
            out_ln(g)
            out_rnorm(g)
            dsa_y(d + 2)
            out_y(g)

            act.wait_ge(products, st["mix_out"][1])
            out_proj("mix_out", 1, FULL, FULL, 1, "up0")

            def ffn(layer, norm):
                w = T - FROM[norm]
                for half in range(2):
                    n = 2 * layer + half
                    if half == 0:
                        fill_x(norm, False, lambda: split_next(f"up{n}", 0, 1, 4, FULL))

                    def mid_hi_of(j, slot):
                        act.wait_ge(mid_ready, HALF * n + j + 1)
                        apart()
                        nc.scalar.activation(mid_hi[:, bass.ds(j * w, w)], ffn_m[:, slot, 0:w], ACT.Copy
                                             ).then_inc(mid_hi_ready, 1)

                    def body(i, last):
                        for s in range(2):
                            j = 2 * i + s
                            first = half == 0 and s == 0 and isinstance(i, int) and i == 0
                            if not first:
                                split_next(f"up{n}", i, 2 * s, 4, FULL)
                            act.wait_ge(drained, st[f"up{n}"][2] + 4 * i + 2 * s + 1)
                            nc.scalar.activation(ffn_g[:, s, 0:w], ffn_g[:, s, 0:w], ACT.Silu).then_inc(gate_silu, 1)
                            if not first:
                                split_next(f"up{n}", i, 2 * s + 1, 4, FFN_W if last and s else FULL)
                            mid_hi_of(j, s)
                    rounds(act, HALF // 2, body, peeled=1 - half)
                    more = layer == 0 or half == 0
                    out_proj(f"down{n}", 2, FFN_W, FULL if more else None, norm + 1 if half else None,
                             "ret_in" if half and layer == 0 else None)

            ffn(0, 2)

            fill_x(4, False, lambda: split_next("ret_in", 0, 1, 12, FULL))
            base, _, tile0 = st["ret_in"]
            act.wait_ge(const1_in, CONSTS1)
            act.wait_ge(rel_in, 16)

            def ret_y(i):
                act.wait_ge(RV.sem, RV.after("y", i))
                apart()
                nc.scalar.activation(mid_hi[:, bass.ds(i * 4 * SEQ, 4 * SEQ)],
                                     ret_sq[:].rearrange("p j t -> p (j t)"), ACT.Copy).then_inc(RA.sem, 1)

            def ret_round(i, last):
                def copy_v(j):
                    act.wait_ge(RP.sem, RP.after(f"vt{j}", i))
                    nc.scalar.activation(v_rows[:, 0:2, j * P:(j + 1) * P],
                                         ps[:, BK_D1, 0:2 * P].rearrange("p (b t) -> p b t", b=2), ACT.Copy)
                    nc.scalar.activation(v_rows[0:16, 2, j * P:(j + 1) * P], ps[0:16, BK_D1, 2 * P:3 * P], ACT.Copy
                                         ).then_inc(RA.sem, 1)

                def silu_g(j):
                    act.wait_ge(drained, tile0 + 12 * i + 8 + j + 1)
                    nc.scalar.activation(ret_g[:, j], ret_g[:, j], ACT.Silu).then_inc(RA.sem, 1)

                for s in range(12):
                    if s > 1 or not (isinstance(i, int) and i == 0):
                        split_next("ret_in", i, s, 12, FULL)
                    if s == 0 and not (isinstance(i, int) and i == 0):
                        ret_y(i - 1)
                    if s == 3:
                        if not (isinstance(i, int) and i == 0):
                            act.wait_ge(RV.sem, RV.after("s2", i - 1))
                            apart()
                        nc.scalar.activation(dmask, rel, ACT.Exp, scale=lg[:, ds1(i)]).then_inc(RA.sem, 1)
                    if s in (6, 7):
                        copy_v(s - 6)
                    if s == 8:
                        copy_v(2)
                    if s == 9:
                        copy_v(3)
                        silu_g(0)
                    if s == 10:
                        silu_g(1)
                        act.wait_ge(RP.sem, RP.after("o", i))
                        nc.scalar.activation(ret_sq[:].rearrange("p j t -> p (j t)"),
                                             ps[:, BK_0:BK_1 + 1].rearrange("p b t -> p (b t)"), ACT.Square
                                             ).then_inc(RA.sem, 1)
                    if s == 11:
                        silu_g(2)
                        act.wait_ge(RP.sem, RP.after("osum", i))
                        nc.scalar.activation(ret_r[:], ps[:, BK_2, 0:SEQ], ACT.Sqrt, scale=1.0 / (4 * P),
                                             bias=eps_col[:, 0:1]).then_inc(RA.sem, 1)
                        silu_g(3)
            ret_round(0, False)
            with act.Fori(1, HEADS) as i:
                ret_round(i, False)
            ret_y(HEADS - 1)
            out_proj("ret_out", 2, FULL, FULL, 5, "up2")
            ffn(1, 6)

        @block.vector
        def _(dve):
            V = nc.vector

            def split_lo(slot, width, piece, start=0, end=2):
                for b, (cut, count) in enumerate(halves(width)):
                    if start <= b < end:
                        dve.wait_ge(hi_ready, 2 * piece + b + 1)
                        V.tensor_tensor(w_lo[:, slot, cut], raw[:, slot, cut], w_hi[:, slot, cut],
                                        ALU.subtract).then_inc(lo_ready, count)

            def split_next(stage, i, q, per_round, width):
                split_lo((q + 1) % 2, width, st[stage][0] + per_round * i + q + 1)

            def take_r(norm, dst):
                t0 = FROM[norm]
                dve.wait_ge(rooted, norm + 1)
                V.reciprocal(dst[:, t0:T], dst[:, t0:T]).then_inc(r_ready, 1)
                dve.wait_ge(r_ready, norm + 1)

            def fill_x(norm, piece=None):
                t0 = FROM[norm]
                if norm == 0:
                    for k in range(KC):
                        if k == 8:
                            split_lo(1, FULL, 1)
                        x_low(norm, k)
                    split_lo(0, FULL, 2)
                else:
                    split_lo(1, FULL, piece, 0, 1)
                    take_r(norm - 1, r_post)
                    for k in range(4):
                        scale(norm - 1, k)
                        if k == 1:
                            split_lo(1, FULL, piece, 1)
                    with dve.Fori(0, KC - 4) as k:
                        scale(norm - 1, k + 4)
                        x_low(norm, k)
                    for k in range(KC - 4, KC):
                        x_low(norm, k)
                    split_lo(0, FULL, piece + 1)
                take_r(norm, r_pre)

            def x_low(norm, k):
                t0 = FROM[norm]
                dve.wait_ge(x_hi_ready, KC * (norm // 2) + k + 1)
                V.scalar_tensor_tensor(x_lo[:, ds1(k), t0:T], h[:, ds1(k), t0:T], gains[:, norm, ds1(k)],
                                       x_hi[:, ds1(k), t0:T], ALU.mult, ALU.subtract).then_inc(x_lo_ready, 1)

            def scale(norm, k):
                t0 = FROM[norm]
                V.scalar_tensor_tensor(u[:, ds1(k), t0:T], u[:, ds1(k), t0:T], gains[:, norm, ds1(k)],
                                       r_post[:, t0:T], ALU.mult, ALU.mult).then_inc(scaled, 1)

            def out_proj(stage, n_sub, width, next_width, t0, add, norm):
                _, sig, _ = st[stage]

                def body(i, last):
                    for s in range(2):
                        for sub in range(n_sub):
                            q = n_sub * s + sub
                            w = next_width if last and q == 2 * n_sub - 1 else width
                            if w:
                                split_next(stage, i, q, 2 * n_sub, w)
                        dve.wait_ge(products, sig + 4 * n_sub * i + 2 * n_sub * (s + 1))
                        dst = u[:, ds1(2 * i + s), t0:T]
                        if add:
                            V.tensor_tensor(dst, dst, ps[:, s, t0:T], ALU.add).then_inc(drained, 1)
                        else:
                            V.tensor_copy(dst, ps[:, s, t0:T]).then_inc(drained, 1)
                rounds(dve, 8, body)
            dve.wait_ge(gains_in, 16)
            dve.wait_ge(cleared, 1)
            split_lo(0, FULL, 0)
            fill_x(0)
            for q in range(8):
                if q > 1:
                    split_lo((q + 1) % 2, FULL, q + 1)
                dve.wait_ge(products, 2 * q + 2)
                V.tensor_tensor(lat[:, q], ps[:, q % 2 if q > 1 else BK_0 + q, 0:T], r_pre[:], ALU.mult
                                ).then_inc(drained, 1)

            def split_lo_part(i, s, parts):
                piece = head_at(i)[0]
                w = 4 * P if s == 4 and not (isinstance(i, int) and i < LAG - 1) else FULL
                for p in parts:
                    if w < FULL:
                        if p == 0:
                            split_lo(s % 2, w, piece + s)
                        continue
                    if p % 2 == 0:
                        dve.wait_ge(hi_ready, 2 * (piece + s) + p // 2 + 1)
                    cut = slice(p * w // 4, (p + 1) * w // 4)
                    done = V.tensor_tensor(w_lo[:, s % 2, cut], raw[:, s % 2, cut], w_hi[:, s % 2, cut],
                                           ALU.subtract)
                    if p % 2:
                        done.then_inc(lo_ready, 1)

            def take_tile(i, s):
                _, sig, _, _ = head_at(i)
                first = isinstance(i, int) and i == 0
                dve.wait_ge(products, sig + 2 * s + 2)
                if s < 3:
                    V.tensor_tensor(conv_in[:, s, 3:3 + T], ps[:, s % 2, 0:T], r_pre[:], ALU.mult
                                    ).then_inc(drained, 1)
                else:
                    if not first:
                        dve.wait_ge(CA.sem, CA.after("gate", i - 1))
                    V.tensor_tensor(r_post[:], ps[:, s % 2, 0:T], r_pre[:], ALU.mult).then_inc(drained, 1)

            def conv(i, s, taps):
                for k in taps:
                    if k == 0:
                        dve.wait_ge(drained, head_at(i)[2] + s + 1)
                        if not (isinstance(i, int) and i == 0):
                            dve.wait_ge(CA.sem, CA.after(f"silu{s}", i - 1))
                        V.tensor_scalar(conv_acc[:, s], conv_in[:, s, 0:T], conv_w[:, ds1(i), s, 0:1], None,
                                        ALU.mult).then_inc(CV.sem, 1)
                    else:
                        dve.wait_ge(CV.sem, CV.after(f"t{s}{k - 1}", i))
                        V.scalar_tensor_tensor(conv_acc[:, s], conv_in[:, s, k:k + T], conv_w[:, ds1(i), s, k:k + 1],
                                               conv_acc[:, s], ALU.mult, ALU.add).then_inc(CV.sem, 1)

            split_lo_part(0, 1, range(4))
            dve.wait_ge(const_in, CONSTS0)
            dve.wait_ge(LA.sem, LA.after("rooted"))
            V.reciprocal(kq[:, 1:4, 0:T], kq[:, 1:4, 0:T]).then_inc(LV.sem, 1)
            take_tile(0, 0)
            split_lo_part(0, 2, range(4))
            dve.wait_ge(LV.sem, LV.after("recip"))
            for k in range(4):
                last = V.scalar_tensor_tensor(lat[:, k], lat[:, k], lat_gain[:, k:k + 1], kq[:, 1, 0:T],
                                              ALU.mult, ALU.mult)
            last.then_inc(LV.sem, 1)
            V.scalar_tensor_tensor(kidx[:], lat[:, 6], lat_gain[:, 6:7], kq[:, 3, 0:T], ALU.mult, ALU.mult)
            for k in range(4, 6):
                last = V.scalar_tensor_tensor(lat[:, k], lat[:, k], lat_gain[:, k:k + 1], kq[:, 2, 0:T],
                                              ALU.mult, ALU.mult)
            last.then_inc(LV.sem, 1)
            dve.wait_ge(LA.sem, LA.after("hi_kv"))
            V.tensor_tensor(cq_lo[:], lat[:, 0:4], cq_hi[:], ALU.subtract)
            V.tensor_tensor(ckv_lo[:, :, 0:T], lat[:, 4:6], ckv_hi[:, :, 0:T], ALU.subtract).then_inc(LV.sem, 1)
            take_tile(0, 1)
            split_lo_part(0, 3, range(4))
            conv(0, 0, range(4))
            V.tensor_copy(gsel[:, 0, 0:T], lat[64:64 + HEADS, 7])
            V.tensor_copy(gb8[:, 1, 0:T], lat[32:32 + HEADS, 7]).then_inc(LV.sem, 1)
            dve.wait_ge(LV.sem, LV.after("shifted"))
            V.tensor_scalar(gsel[:, 0, 0:T], gsel[:, 0, 0:T], decay8[:, 1:2], None, ALU.add).then_inc(LV.sem, 1)
            dve.wait_ge(LV.sem, LV.after("dt"))
            V.tensor_scalar(gb8[:, 0, 0:T], gsel[:, 0, 0:T], 0.0, None, ALU.max).then_inc(LV.sem, 1)
            V.scalar_tensor_tensor(gsel[:, 1, 0:T], gsel[:, 0, 0:T], -1.0, gsel[:, 0, 0:T], ALU.mult, ALU.min
                                   ).then_inc(LV.sem, 1)
            dve.wait_ge(LA.sem, LA.after("beta_exp"))
            V.tensor_scalar(gb8[:, 1, 0:T], gb8[:, 1, 0:T], 1.0, None, ALU.add).then_inc(LV.sem, 1)
            dve.wait_ge(LV.sem, LV.after("one"))
            V.reciprocal(gb8[:, 1, 0:T], gb8[:, 1, 0:T]).then_inc(LV.sem, 1)
            dve.wait_ge(LA.sem, LA.after("ln"))
            V.tensor_tensor(gb8[:, 0, 0:T], gb8[:, 0, 0:T], gsel[:, 1, 0:T], ALU.add).then_inc(LV.sem, 1)
            dve.wait_ge(LA.sem, LA.after("a_exp"))
            V.tensor_scalar(decay8[:, 3:4], decay8[:, 2:3], -1.0, None, ALU.mult).then_inc(LV.sem, 1)
            dve.wait_ge(LV.sem, LV.after("nea"))
            V.tensor_scalar(gsel[:, 0, 0:T], gb8[:, 0, 0:T], decay8[:, 3:4], None, ALU.mult).then_inc(LV.sem, 1)
            dve.wait_ge(LV.sem, LV.after("decay"))
            for n in range(NCH):
                c = slice(n * CH, (n + 1) * CH)
                V.tensor_tensor_scan(gb8[:, 0, c], ones[0:HEADS, 0:CH], gsel[:, 0, c], 0.0, ALU.mult, ALU.add
                                     ).then_inc(LV.sem, 1)
            dve.wait_ge(LP_.sem, LP_.after("index_w"))
            w_scale = (IDX_HEADS * IDX_DIM) ** -0.5
            V.tensor_scalar(widx[:, 0:2], ps[:, BK_3, 0:32].rearrange("p (b t) -> p b t", b=2), w_scale, None,
                            ALU.mult)
            V.tensor_scalar(widx[0:16, 2], ps[0:16, BK_3, 32:48], w_scale, None, ALU.mult).then_inc(LV.sem, 1)
            conv(0, 1, range(4))

            take_tile(0, 2)
            conv(0, 2, range(4))
            split_lo_part(0, 4, range(4))
            take_tile(0, 3)
            split_lo(1, FULL, INDEX_Q[0] + 1)
            for t in range(8):
                if t == 4:
                    split_lo(0, FULL, INDEX_Q[0] + 2)
                dve.wait_ge(products, INDEX_Q[1] + t + 1)
                V.tensor_copy(q_index[:, t], ps[:, t % 2, 0:T]).then_inc(drained, 1)
            dve.wait_ge(LP_.sem, LP_.after("columns"))
            V.tensor_copy(cols[:, 0:2].rearrange("p a n t -> p (a n t)"), ps[0:CH, BK_2, 0:2 * NCH * HEADS]
                          ).then_inc(LV.sem, 1)
            dve.wait_ge(LA.sem, LA.after("decayed"))
            V.tensor_tensor(cols[:, 3], cols[:, 1], cols[:, 2], ALU.mult).then_inc(LV.sem, 1)

            def index_pair(i, slot):
                if not isinstance(i, int) or i not in (1, 2):
                    return
                for c in range(2 * slot, 2 * slot + 2):
                    if i == 2 and slot >= 8:
                        break
                    c += 2 * IDX_HEADS * (i - 1)
                    b, n_head = divmod(c, IDX_HEADS)
                    n, (c0, keys) = BLK[b][1], ROW[b]
                    acc = bias[0:n, c0:c0 + keys]
                    dve.wait_ge(relued, c + 1)
                    one, w = dsa_s[0:n, T * (c % 2):T * (c % 2) + keys], widx[0:n, b, n_head:n_head + 1]
                    if n_head == 0:
                        V.tensor_scalar(acc, one, w, None, ALU.mult).then_inc(scored, 1)
                    else:
                        dve.wait_ge(scored, c)
                        V.scalar_tensor_tensor(acc, one, w, acc, ALU.mult, ALU.add).then_inc(scored, 1)
                b = 2 * (i - 1) + slot // 8 - 1
                m = slot % 8
                if b < 0:
                    return
                n, (c0, keys) = BLK[b][1], ROW[b]
                acc = bias[0:n, c0:c0 + keys]
                if m == 0:
                    dve.wait_ge(causal, b + 1)
                else:
                    dve.wait_ge(TV.sem, TV.after(f"r{m - 1}", b))
                V.max(top8[0:n, :], acc).then_inc(TV.sem, 1)
                dve.wait_ge(TV.sem, TV.after(f"m{m}", b))
                V.match_replace(acc, top8[0:n, :], acc, TAKEN).then_inc(TV.sem, 1)
                if m == TOPK // 8 - 1:
                    dve.wait_ge(TV.sem, TV.after(f"r{m}", b))
                    V.tensor_scalar(acc, acc, TAKEN_EDGE, MASKED, ALU.is_gt, ALU.mult).then_inc(TV.sem, 1)

            def dsa_lo(i, s, width):
                split_lo(s % 2, width, dsa_at(i)[0] + s)

            def dsa_take_q(i):
                dve.wait_ge(products, dsa_at(i)[1] + 1)
                V.tensor_copy(q_h, ps[:, 0, 0:T]).then_inc(drained, 1)

            def dsa_take_k(i):
                dve.wait_ge(products, dsa_at(i)[1] + 2)
                V.tensor_copy(k_h, ps[:, 1, 0:T]).then_inc(drained, 1)

            def dsa_score(i):
                dve.wait_ge(DP.sem, DP.after("logits", i))
                for b, (q0, n) in enumerate(BLK):
                    c0, keys = ROW[b]
                    src = ps[0:n, BK_D0, 128 * b:128 * b + keys] if b < 2 else ps[0:n, BK_D1, 0:keys]
                    last = V.scalar_tensor_tensor(dsa_s[0:n, c0:c0 + keys], src, P ** -0.5, bias[0:n, c0:c0 + keys],
                                                  ALU.mult, ALU.add)
                last.then_inc(DV.sem, 1)
                dve.wait_ge(DV.sem, DV.after("scored", i))
                for b, (q0, n) in enumerate(BLK):
                    c0, keys = ROW[b]
                    last = V.tensor_reduce(mx[0:n, b:b + 1], dsa_s[0:n, c0:c0 + keys], AX.X, ALU.max, negate=True)
                last.then_inc(DV.sem, 1)

            def dsa_recip(i):
                dve.wait_ge(DA.sem, DA.after("exped", i))
                V.reciprocal(rinv[:, 0:2], rs[:, 0:2])
                V.reciprocal(rinv[0:16, 2:3], rs[0:16, 2:3]).then_inc(DV.sem, 1)

            def dsa_y(i):
                dve.wait_ge(DA.sem, DA.after("y_hi", i))
                V.tensor_tensor(y_lo[:, ds1(i), :], ps[:, BK_D1, 0:T], y_hi[:, ds1(i), :], ALU.subtract
                                ).then_inc(DV.sem, 1)

            def over(ap2, width):
                return ap2.to_broadcast([CH, NCH, width])

            def each(ap2):
                return ap2.unsqueeze(1).to_broadcast([CH, NCH, CH])

            def bank(b):
                return ps[0:CH, b, 0:LP].rearrange("p (n t) -> p n t", n=NCH)

            def rows(b):
                return ps[0:CH, b, 0:NCH * P].rearrange("p (n t) -> p n t", n=NCH)

            def gdn_select(i):
                V.tensor_scalar(gsel[:], gb8[:], ident[0:HEADS, ds1(i)], None, ALU.mult).then_inc(GV.sem, 1)

            def gdn_kq(i):
                dve.wait_ge(GA.sem, GA.after("rnorm", i))
                V.tensor_tensor(kq[:, 0, 0:T], qkv[:, 1, 0:T], kq[:, 3, 0:T], ALU.mult)
                V.scalar_tensor_tensor(kq[:, 1, 0:T], qkv[:, 0, 0:T], P ** -0.5, kq[:, 2, 0:T], ALU.mult, ALU.mult
                                       ).then_inc(GV.sem, 1)

            def gdn_kb(i):
                dve.wait_ge(GV.sem, GV.after("kq", i))
                dve.wait_ge(GA.sem, GA.after("decayed", i))
                V.tensor_tensor(kq[:, 2], kq[:, 0], ps[:, BK_3, 0:LP], ALU.mult)
                V.tensor_tensor(kq[:, 3], kq[:, 1], dec[:], ALU.mult).then_inc(GV.sem, 1)

            def gdn_arg(i):
                for n in range(NCH):
                    V.tensor_scalar(at_l[:, n], ps[0:CH, BK_2, n * CH:(n + 1) * CH], cols[:, 0, n, ds1(i)], 0.0,
                                    ALU.subtract, ALU.min)
                V.tensor_tensor(kd_last[:].unsqueeze(2), bank(BK_2)[:, :, CH - 1:CH], cols[:, 0, :, ds1(i)],
                                ALU.subtract).then_inc(GV.sem, 1)

            def gdn_mask(i):
                dve.wait_ge(GA.sem, GA.after("decmat", i))
                V.tensor_tensor(at_l, at_l, each(upto[:]), ALU.mult).then_inc(GV.sem, 1)

            def gdn_mats(i):
                dve.wait_ge(GP.sem, GP.after("scores", i))
                dve.wait_ge(GV.sem, GV.after("masked", i))
                V.tensor_tensor(at, bank(BK_0), at_l, ALU.mult)
                V.tensor_tensor(qk, bank(BK_1), at_l, ALU.mult).then_inc(GV.sem, 1)

            def gdn_rows(i):
                dve.wait_ge(GP.sem, GP.after("turned", i))
                V.tensor_tensor(kbg, rows(BK_2), over(cols[:, 3, :, ds1(i)], P), ALU.mult)
                V.tensor_tensor(kd, rows(BK_2), over(kd_last[:].unsqueeze(2), P), ALU.mult)
                V.tensor_tensor(vb, rows(BK_3), over(cols[:, 1, :, ds1(i)], P), ALU.mult).then_inc(GV.sem, 1)

            def gdn_tt0(i):
                dve.wait_ge(GV.sem, GV.after("mats", i))
                V.tensor_tensor(at_l, at, each(levels[:, 0]), ALU.mult).then_inc(GV.sem, 1)
                dve.wait_ge(GV.sem, GV.after("at0", i))
                V.tensor_tensor(tt, each(ident[0:CH, 0:CH]), at_l, ALU.subtract).then_inc(GV.sem, 1)

            def gdn_level(i, l):
                if l < LEVELS - 1:
                    dve.wait_ge(GP.sem, GP.after(f"z{l}", i))
                    V.tensor_tensor(tm, tm, bank(BK_0), ALU.subtract).then_inc(GV.sem, 1)
                dve.wait_ge(GP.sem, GP.after(f"zt{l}", i))
                V.tensor_tensor(tt, tt, bank(BK_2), ALU.subtract).then_inc(GV.sem, 1)

            def gdn_state(i, n):
                dve.wait_ge(GP.sem, GP.after(f"k{n}", i))
                if n == 0:
                    V.tensor_copy(state[:], ps[:, BK_2, 0:P]).then_inc(GV.sem, 1)
                else:
                    V.scalar_tensor_tensor(state[:], state[:], dec[:, (n + 1) * CH - 1:(n + 1) * CH],
                                           ps[:, BK_2, 0:P], ALU.mult, ALU.add).then_inc(GV.sem, 1)

            def out_gate(i):
                dve.wait_ge(FA.sem, FA.after("rnorm", i))
                V.tensor_tensor(o_m, o_m, o_sq, ALU.mult).then_inc(FV.sem, 1)
                dve.wait_ge(CA.sem, CA.after("gate", i))
                dve.wait_ge(FV.sem, FV.after("om0", i))
                V.tensor_tensor(o_m, o_m, gate[:], ALU.mult).then_inc(FV.sem, 1)

            def out_y(i):
                dve.wait_ge(FA.sem, FA.after("y_hi", i))
                V.tensor_tensor(y_lo[:, ds1(i + HEADS), :], o_m, y_hi[:, ds1(i + HEADS), :], ALU.subtract
                                ).then_inc(FV.sem, 1)

            def mixer_body(i, g, f, d):
                if d is not None:
                    dsa_lo(d, 1, 4 * P)
                    dsa_take_q(d)
                if g is not None:
                    gdn_select(g)
                if d is not None:
                    dsa_take_k(d)
                    dsa_lo(d, 2, FULL)
                if f is not None:
                    out_gate(f)
                if g is not None:
                    gdn_kq(g)
                    gdn_kb(g)
                    gdn_arg(g)
                index_pair(i, 0)
                if f is not None:
                    out_y(f)
                if d is not None:
                    dsa_score(d)
                split_lo_part(i, 1, (0, 1))
                index_pair(i, 1)
                if g is not None:
                    gdn_mask(g)
                    gdn_mats(g)
                if d is not None:
                    dsa_recip(d)
                if g is not None:
                    gdn_tt0(g)
                split_lo_part(i, 1, (2, 3))
                index_pair(i, 2)
                if g is not None:
                    gdn_rows(g)
                index_pair(i, 3)
                take_tile(i, 0)
                conv(i, 0, range(4))
                index_pair(i, 4)
                if g is not None:
                    gdn_level(g, 1)
                split_lo_part(i, 2, (0, 1))
                if d is not None:
                    dsa_y(d)
                index_pair(i, 5)
                if g is not None:
                    gdn_level(g, 2)
                split_lo_part(i, 2, (2, 3))
                index_pair(i, 6)
                if g is not None:
                    gdn_level(g, 3)
                index_pair(i, 7)
                take_tile(i, 1)
                conv(i, 1, (0, 1))
                if g is not None:
                    gdn_level(g, 4)
                conv(i, 1, (2, 3))
                index_pair(i, 8)
                if g is not None:
                    gdn_level(g, 5)
                split_lo_part(i, 3, (0, 1))
                index_pair(i, 9)
                if g is not None:
                    gdn_level(g, 6)
                split_lo_part(i, 3, (2, 3))
                index_pair(i, 10)
                index_pair(i, 11)
                take_tile(i, 2)
                if g is not None:
                    gdn_state(g, 0)
                conv(i, 2, range(4))
                index_pair(i, 12)
                index_pair(i, 13)
                if g is not None:
                    gdn_state(g, 1)
                split_lo_part(i, 4, range(4))
                index_pair(i, 14)
                index_pair(i, 15)
                take_tile(i, 3)

            mixer_body(1, 0, None, None)
            mixer_body(2, 1, 0, None)
            dve.wait_ge(bias_done, 3)
            with dve.Fori(0, HEADS - LAG) as i:
                mixer_body(i + 3, i + 2, i + 1, i)

            g, d = HEADS - 1, HEADS - LAG
            dsa_lo(d, 1, 4 * P)
            dsa_take_q(d)
            gdn_select(g)
            dsa_take_k(d)
            dsa_lo(d, 2, 4 * P)
            out_gate(g - 1)
            gdn_kq(g)
            gdn_kb(g)
            gdn_arg(g)
            out_y(g - 1)
            dsa_score(d)
            gdn_mask(g)
            gdn_mats(g)
            gdn_tt0(g)
            dsa_recip(d)
            gdn_rows(g)
            dsa_lo(d + 1, 1, 4 * P)
            gdn_level(g, 1)
            dsa_y(d)
            dsa_take_q(d + 1)
            dsa_lo(d + 1, 2, 4 * P)
            dsa_take_k(d + 1)
            gdn_level(g, 2)
            dsa_score(d + 1)
            gdn_level(g, 3)
            dsa_recip(d + 1)
            dsa_lo(d + 2, 1, 4 * P)
            gdn_level(g, 4)
            gdn_level(g, 5)
            gdn_level(g, 6)
            dsa_y(d + 1)
            dsa_take_q(d + 2)
            dsa_lo(d + 2, 2, FULL)
            dsa_take_k(d + 2)
            gdn_state(g, 0)
            dsa_score(d + 2)
            gdn_state(g, 1)
            dsa_recip(d + 2)
            dsa_y(d + 2)
            out_gate(g)
            out_y(g)

            out_proj("mix_out", 1, FULL, FULL, 0, False, 1)

            def ffn(layer, norm):
                t0 = FROM[norm]
                w = T - t0
                for half in range(2):
                    n = 2 * layer + half
                    if half == 0:
                        fill_x(norm, st[f"up{n}"][0] + 1)
                    _, sig, _ = st[f"up{n}"]

                    def body(i, last):
                        for s in range(2):
                            j = 2 * i + s
                            first = half == 0 and s == 0 and isinstance(i, int) and i == 0
                            b0 = BK_0 if first else 0
                            if not first:
                                split_next(f"up{n}", i, 2 * s, 4, FULL)
                            dve.wait_ge(products, sig + 8 * i + 4 * s + 2)
                            V.tensor_tensor(ffn_g[:, s, 0:w], ps[:, b0, t0:T], r_pre[:, t0:T], ALU.mult
                                            ).then_inc(drained, 1)
                            if not first:
                                split_next(f"up{n}", i, 2 * s + 1, 4, FFN_W if last and s else FULL)
                            dve.wait_ge(products, sig + 8 * i + 4 * s + 4)
                            V.tensor_tensor(ffn_m[:, s, 0:w], ps[:, b0 + 1, t0:T], r_pre[:, t0:T], ALU.mult
                                            ).then_inc(drained, 1)
                            dve.wait_ge(drained, st[f"up{n}"][2] + 4 * i + 2 * s + 2)
                            dve.wait_ge(gate_silu, HALF * n + j + 1)
                            V.tensor_tensor(ffn_m[:, s, 0:w], ffn_m[:, s, 0:w], ffn_g[:, s, 0:w], ALU.mult
                                            ).then_inc(mid_ready, 1)
                            dve.wait_ge(mid_hi_ready, HALF * n + j + 1)
                            V.tensor_tensor(mid_lo[:, bass.ds(j * w, w)], ffn_m[:, s, 0:w],
                                            mid_hi[:, bass.ds(j * w, w)], ALU.subtract).then_inc(mid_lo_ready, 1)
                    rounds(dve, HALF // 2, body, peeled=1 - half)
                    more = layer == 0 or half == 0
                    out_proj(f"down{n}", 2, FFN_W, FULL if more else None, t0, half == 1,
                             norm + 1 if half else None)

            ffn(0, 2)

            fill_x(4, st["ret_in"][0] + 1)
            dve.wait_ge(const1_in, CONSTS1)
            for c in range(2):
                last = V.tensor_tensor(rope[:, c], rope[:, c], r_pre[:], ALU.mult)
            last.then_inc(rope_ready, 1)
            dve.wait_ge(rope_ready, 1)
            base, sig, tile0 = st["ret_in"]

            def ret_finish(i):
                dve.wait_ge(RV.sem, RV.after("recip", i))
                dve.wait_ge(RA.sem, RA.after("g3", i))
                V.tensor_tensor(ret_g, ret_g, ret_r[:].unsqueeze(1).to_broadcast([P, 4, SEQ]), ALU.mult
                                ).then_inc(RV.sem, 1)
                dve.wait_ge(RV.sem, RV.after("gr", i))
                dve.wait_ge(RP.sem, RP.after("osum", i))
                V.tensor_tensor(ret_sq[:].rearrange("p j t -> p (j t)"),
                                ps[:, BK_0:BK_1 + 1].rearrange("p b t -> p (b t)"),
                                ret_g.rearrange("p j t -> p (j t)"), ALU.mult).then_inc(RV.sem, 1)
                dve.wait_ge(RA.sem, RA.after("y_hi", i))
                V.tensor_tensor(mid_lo[:, bass.ds(i * 4 * SEQ, 4 * SEQ)], ret_sq[:].rearrange("p j t -> p (j t)"),
                                mid_hi[:, bass.ds(i * 4 * SEQ, 4 * SEQ)], ALU.subtract).then_inc(RV.sem, 1)

            def ret_round(i):
                first = isinstance(i, int) and i == 0
                for s in range(12):
                    if s > 1 or not first:
                        split_next("ret_in", i, s, 12, FULL)
                    if s == 0 and not first:
                        ret_finish(i - 1)
                    if s == 11:
                        dve.wait_ge(RA.sem, RA.after("rooted", i))
                        V.reciprocal(ret_r[:], ret_r[:]).then_inc(RV.sem, 1)
                    dve.wait_ge(products, sig + 24 * i + 2 * s + 2)
                    t0 = META if s < 2 else 0
                    tile = ps[:, s + BK_0 if first and s < 2 else s % 2, t0:T]
                    if s in (0, 2):
                        if s == 2:
                            dve.wait_ge(RG.sem, RG.after("q", i))
                        elif not first:
                            dve.wait_ge(RG.sem, RG.after("k", i - 1))
                        V.tensor_tensor(rot_a[:, 0, t0:T], tile, rope[:, 0, t0:T], ALU.mult)
                        V.tensor_tensor(rot_a[:, 1, t0:T], tile, rope[:, 1, t0:T], ALU.mult).then_inc(drained, 1)
                    elif s in (1, 3):
                        dst = q_rot if s == 1 else k_rot
                        V.tensor_tensor(dst[:, 0], tile, rope[:, 1, t0:T], ALU.mult)
                        V.tensor_tensor(dst[:, 1], tile, rope[:, 0, t0:T], ALU.mult).then_inc(drained, 1)
                    elif s < 8:
                        if s > 4:
                            dve.wait_ge(RP.sem, RP.after(f"vt{s - 5}", i))
                        V.tensor_tensor(v_t, tile, r_pre[:], ALU.mult).then_inc(drained, 1)
                    else:
                        V.tensor_tensor(ret_g[:, s - 8], ps[:, s % 2, META:T], r_pre[:, META:T], ALU.mult
                                        ).then_inc(drained, 1)
                    if s == 8:
                        dve.wait_ge(RP.sem, RP.after("scores", i))
                        dve.wait_ge(RA.sem, RA.after("dmask", i))
                        V.scalar_tensor_tensor(ret_s[:, 0:400], ps[:, BK_D0, 0:400], (2 * P) ** -0.5, dmask[:, 0:400],
                                               ALU.mult, ALU.mult).then_inc(RV.sem, 1)
                        V.scalar_tensor_tensor(ret_s[0:16, 400:416], ps[0:16, BK_D0, 400:416], (2 * P) ** -0.5,
                                               dmask[0:16, 400:416], ALU.mult, ALU.mult).then_inc(RV.sem, 1)
            ret_round(0)
            with dve.Fori(1, HEADS) as i:
                ret_round(i)
            ret_finish(HEADS - 1)
            out_proj("ret_out", 2, FULL, FULL, META, False, 5)
            ffn(1, 6)
            take_r(7, r_post)
            with dve.Fori(0, KC) as k:
                scale(7, k)

        @block.gpsimd
        def _(pool):
            G = nc.gpsimd
            G.memset(eps_col[:, 0:1], EPS)
            G.memset(eps_col[:, 1:2], 1.0)
            G.memset(scratch[:], 1.0)
            G.memset(ckv_hi[:, :, T:3 * P].bitcast(F32), 0.0)
            G.memset(ckv_lo[:, :, T:3 * P].bitcast(F32), 0.0)
            G.memset(conv_in[:, :, 0:3], 0.0)
            G.memset(qkv[:, :, T:LP], 0.0)
            G.memset(kq[:, 0:2, T:LP], 0.0)
            G.memset(gb8[:, :, T:LP], 0.0)
            G.memset(gsel[:, :, T:LP], 0.0).then_inc(cleared, 1)

            def hide_later(b):
                q0, n = BLK[b]
                acc = bias[0:n, ROW[b][0]:ROW[b][0] + ROW[b][1]]
                pool.wait_ge(scored, IDX_HEADS * (b + 1))
                G.affine_select(out=acc, in_=acc, pattern=[[-1, ROW[b][1]]], compare_op=ALU.is_ge, fill=NONCAUSAL,
                                base=q0, channel_multiplier=1).then_inc(causal, 1)

            def finish_bias(b):
                q0, n = BLK[b]
                acc = bias[0:n, ROW[b][0]:ROW[b][0] + ROW[b][1]]
                pool.wait_ge(TV.sem, TV.after("chosen", b))
                G.affine_select(out=acc, in_=acc, pattern=[[-1, ROW[b][1]]], compare_op=ALU.is_ge, fill=MASKED,
                                base=q0, channel_multiplier=1).then_inc(bias_done, 1)

            def level(i, l):
                if l == 1:
                    pool.wait_ge(GV.sem, GV.after("tt0", i))
                else:
                    pool.wait_ge(GP.sem, GP.after(f"y{l - 1}", i))
                G.tensor_tensor(at_l, at, levels[:, l].unsqueeze(1).to_broadcast([CH, NCH, CH]), ALU.mult
                                ).then_inc(GG.sem, 1)

            for l in range(1, LEVELS):
                if l == 5:
                    hide_later(0)
                level(0, l)
            hide_later(1)
            for l in range(1, LEVELS):
                if l == 2:
                    finish_bias(0)
                if l == 5:
                    hide_later(2)
                    finish_bias(1)
                level(1, l)
            finish_bias(2)
            with pool.Fori(2, HEADS) as i:
                for l in range(1, LEVELS):
                    level(i, l)

            def residual(norm):
                t0 = FROM[norm]
                with pool.Fori(0, KC) as k:
                    pool.wait_ge(scaled, KC * (norm // 2) + k + 1)
                    G.tensor_tensor(h[:, ds1(k), t0:T], h[:, ds1(k), t0:T], u[:, ds1(k), t0:T], ALU.add
                                    ).then_inc(h_ready, 1)

            def square_sum(norm):
                t0 = FROM[norm]

                def add(k, slot):
                    pool.wait_ge(squared, KC * norm + k + 1)
                    if isinstance(k, int) and k == 0:
                        G.tensor_copy(sq_sum[:, t0:T], sq[:, slot, t0:T]).then_inc(summed, 1)
                    else:
                        pool.wait_ge(summed, KC * norm + k)
                        G.tensor_tensor(sq_sum[:, t0:T], sq_sum[:, t0:T], sq[:, slot, t0:T], ALU.add
                                        ).then_inc(summed, 1)

                add(0, 0)
                add(1, 1)
                with pool.Fori(1, KC // 2) as i:
                    for s in range(2):
                        add(2 * i + s, s)

            square_sum(1)
            residual(1)
            square_sum(3)
            residual(3)
            pool.wait_ge(h_ready, 2 * KC)
            pool.dma_start(rel, a["rel"]).then_inc(rel_in, 16)
            _, _, tile0 = st["ret_in"]
            with pool.Fori(0, HEADS) as i:
                for s, (dst, t0) in enumerate(((q_rot, META), (k_rot, 0))):
                    pool.wait_ge(drained, tile0 + 12 * i + 2 * s + 2)
                    G.tensor_tensor(dst[:, 0], rot_a[:, 0, t0:T], dst[:, 0], ALU.subtract)
                    G.tensor_tensor(dst[:, 1], rot_a[:, 1, t0:T], dst[:, 1], ALU.add).then_inc(RG.sem, 1)
            square_sum(5)
            residual(5)
            square_sum(7)
            residual(7)


def tiles16(w):
    k, m = w.shape
    return w.reshape(k // P, P, m // P, P).transpose(2, 1, 0, 3).reshape(m // P, P, k // P * P)


def by_chunk(v):
    return v.reshape(-1, P).T


def kernel(**inputs):
    import concourse.bacc as bacc
    from concourse.bass_utils import run_bass_kernel_spmd

    g = {k: np.asarray(v) for k, v in inputs.items()}
    w_in = g["hy_w_in"][0]
    cut = np.cumsum([512, 256, IDX_DIM, IDX_HEADS, 3 * 1024, 1024, HEADS, HEADS])
    c_q, c_kv, k_idx, w_idx, qkv, z, beta, a_raw = np.split(w_in, cut[:-1], axis=1)
    zero = np.zeros((D, P), np.float32)
    rest = zero.copy()
    rest[:, 0:16], rest[:, 32:40], rest[:, 64:72] = w_idx, beta, a_raw
    arrays = {
        "x_t": np.concatenate([g["meta_tokens"], g["x"][0]], 0).T.reshape(KC, P, T).transpose(1, 0, 2),
        "w_latent": tiles16(np.concatenate([c_q, c_kv, k_idx, k_idx, rest], 1)),
    }
    arrays["w_index_q"] = tiles16(g["dsa_w_qidx"][0]).reshape(2, 4, P, 4 * P).transpose(0, 2, 1, 3).reshape(2, P, 16 * P)
    parts = [tiles16(m) for m in (qkv[:, :1024], qkv[:, 1024:2048], qkv[:, 2048:], z)]
    arrays["w_heads"] = np.stack(parts, 1).reshape(4 * HEADS, P, 16 * P)
    kv = tiles16(g["dsa_w_ukv"][0]).reshape(HEADS, 2, P, 2 * P).transpose(0, 2, 1, 3).reshape(HEADS, P, 4 * P)
    arrays["w_dsa"] = np.stack([tiles16(g["dsa_w_uq"][0]), kv], 1).reshape(2 * HEADS, P, 4 * P)
    arrays["w_mix_out"] = tiles16(g["hy_w_out"][0])
    up, down = [], []
    for layer in range(2):
        gate_up = np.stack([tiles16(g["ffn_w_gate"][layer]), tiles16(g["ffn_w_up"][layer])], 1)
        up.append(gate_up.reshape(4 * HALF, P, 16 * P))
        wd = tiles16(g["ffn_w_down"][layer]).reshape(KC, P, 2, 2, SUB * P).transpose(2, 0, 3, 1, 4)
        down.append(wd.reshape(4 * KC, P, SUB * P))
    arrays["w_up"], arrays["w_down"] = np.concatenate(up), np.concatenate(down)
    q, k, v, gt = np.split(g["ret_w_in"][0], [D, 2 * D, 2 * D + 4096], axis=1)

    def pairs(m):
        return m.reshape(D, HEADS, P, 2).transpose(0, 1, 3, 2).reshape(D, HEADS, 2 * P)

    ret = np.concatenate([pairs(q), pairs(k), v.reshape(D, HEADS, 512), gt.reshape(D, HEADS, 512)], 2)
    arrays["w_ret_in"] = tiles16(ret.reshape(D, HEADS * 12 * P))
    arrays["w_ret_out"] = tiles16(g["ret_w_out"][0]).reshape(KC, P, 2, KC * P).transpose(0, 2, 1, 3).reshape(2 * KC, P, KC * P)
    norms = [g[n][l] for l in range(2) for n in ("mix_norm_pre", "mix_norm_post", "ffn_norm_pre", "ffn_norm_post")]
    arrays["gains"] = np.stack([by_chunk(n) for n in norms], 1)
    kn = g["dsa_kidx_norm"][0]
    arrays["lat_gain"] = np.concatenate([by_chunk(g["dsa_q_norm"][0]), by_chunk(g["dsa_kv_norm"][0]),
                                         np.concatenate([kn, kn])[:, None], g["gdn_o_norm"][0][:, None]], 1)
    cw = g["gdn_conv_w"][0].reshape(4, 3, HEADS, P)
    arrays["conv_w"] = cw.transpose(3, 2, 1, 0)
    arrays["decay8"] = np.stack([g["gdn_a_log"][0], g["gdn_dt_bias"][0]], 1)
    arrays["ones"] = np.ones((P, P), np.float32)
    arrays["ident"] = np.eye(P, dtype=np.float32)
    j, i = np.arange(CH)[:, None], np.arange(CH)[None, :]
    arrays["levels"] = np.stack([((i >> l) % 2 == 1) & ((j >> l) == (i >> l) - 1) for l in range(LEVELS)], 1).astype(np.float32)
    arrays["upto"] = (j <= i).astype(np.float32)
    inv = 1.0 / (np.float32(10000.0) ** np.linspace(0.0, 1.0, P, dtype=np.float32))
    ang = np.arange(T, dtype=np.float32)[None, :] * inv.astype(np.float32)[:, None]
    arrays["rope"] = np.stack([np.cos(ang), np.sin(ang)], 1).astype(np.float32)
    log_gamma = np.log(1.0 - 2.0 ** (-5.0 - np.arange(HEADS)))
    arrays["log_gamma"] = np.tile(log_gamma.astype(np.float32), (P, 1))
    rel = np.full((P, 416), 1.0e9, np.float32)
    for (c0, q0, nq), (k0, nk) in zip(RROW, BLK):
        dist = (META + q0 + np.arange(nq))[None, :] - (k0 + np.arange(nk))[:, None]
        rel[:nk, c0:c0 + nq] = np.where(dist >= 0, dist, 1.0e9)
    arrays["rel"] = rel
    arrays = {k: np.ascontiguousarray(v) for k, v in arrays.items()}

    nc = bacc.Bacc("TRN2", target_bir_lowering=False, num_devices=1)
    aps = {k: nc.dram_tensor(f"in_{k}", v.shape, mybir.dt.from_np(v.dtype), kind="ExternalInput").ap()
           for k, v in arrays.items()}
    out = nc.dram_tensor("out_t", (P, KC, SEQ), F32, kind="ExternalOutput").ap()
    trunk(nc, aps, out)
    r = run_bass_kernel_spmd(nc, [{f"in_{k}": v for k, v in arrays.items()}], core_ids=[0])
    res = r.results[0]["out_t"]
    return res.transpose(1, 0, 2).reshape(D, SEQ).T[None]
```
